# Optimizing a Trainium2 kernel written in Bass

```python
import math
import jax, jax.numpy as jnp
from jax import lax
import numpy as np

D_MODEL = 1024
BATCH = 1
SEQ = 256
DEPTH = 2

HEAD_DIM = 64
POOL_WINDOWS = (2, 4, 8, 16)
POOL_GROUPS = 4
POOL_GROUP_DIM = 64
POOL_WIDTH = POOL_GROUPS * POOL_GROUP_DIM
DIFF_HEADS = 4
DIFF_V_DIM = 2 * HEAD_DIM
DIFF_QK_WIDTH = DIFF_HEADS * 2 * HEAD_DIM
DIFF_WIDTH = DIFF_HEADS * DIFF_V_DIM
SB_HEADS = 4
SB_WIDTH = SB_HEADS * HEAD_DIM
FOX_HEADS = 4
FOX_WIDTH = FOX_HEADS * HEAD_DIM
N_BRANCHES = 4
BRANCH_WIDTHS = (POOL_WIDTH, DIFF_WIDTH, SB_WIDTH, FOX_WIDTH)
MIX_WIDTH = POOL_WIDTH + DIFF_WIDTH + SB_WIDTH + FOX_WIDTH
IN_SPLITS = (POOL_WIDTH,
             DIFF_QK_WIDTH, DIFF_QK_WIDTH, DIFF_WIDTH,
             SB_WIDTH, SB_WIDTH, SB_WIDTH,
             FOX_WIDTH, FOX_WIDTH, FOX_WIDTH, FOX_HEADS,
             N_BRANCHES * D_MODEL)
D_IN = sum(IN_SPLITS)
D_FF = -(-(8 * D_MODEL) // (3 * 256)) * 256
Q_BLOCK = 128
ROPE_THETA = 10000.0
NORM_EPS = 1e-6

kernel_name = 'hybrid_gated_parallel_mixers'

def _rms_norm(x, gain):
    xf = x.astype(jnp.float32)
    y = xf * lax.rsqrt(jnp.mean(xf * xf, axis=-1, keepdims=True) + NORM_EPS)
    return (y * gain.astype(jnp.float32)).astype(x.dtype)

def _rope(x, positions):
    half = x.shape[-1] // 2
    inv_freq = ROPE_THETA ** (-jnp.arange(half, dtype=jnp.float32) / half)
    ang = positions.astype(jnp.float32)[:, None] * inv_freq[None, :]
    cos, sin = jnp.cos(ang), jnp.sin(ang)
    xf = x.astype(jnp.float32)
    x1, x2 = xf[..., :half], xf[..., half:]
    return jnp.concatenate([x1 * cos - x2 * sin, x2 * cos + x1 * sin], axis=-1).astype(x.dtype)

def _heads(t, n_heads):
    b, s, _ = t.shape
    return t.reshape(b, s, n_heads, -1).transpose(0, 2, 1, 3)

def _block_positions(i, seq_len):
    q_pos = i * Q_BLOCK + jnp.arange(Q_BLOCK)
    k_pos = jnp.arange(seq_len)
    return q_pos[:, None], k_pos[None, :]

def _sweep_query_blocks(block_fn, seq_len):
    out = lax.map(block_fn, jnp.arange(seq_len // Q_BLOCK))
    n_blocks, b, h, qb, dv = out.shape
    return out.transpose(1, 0, 3, 2, 4).reshape(b, n_blocks * qb, h * dv)

def _diff_lambda_init(layer):
    return 0.8 - 0.6 * math.exp(-0.3 * layer)

def _pool_mixer(u, pool_w, pool_scale):
    b, s, _ = u.shape
    uf = u.reshape(b, s, POOL_GROUPS, POOL_GROUP_DIM).astype(jnp.float32)
    csum = jnp.cumsum(uf, axis=1)
    t = jnp.arange(s)
    outs = []
    for g, w in enumerate(POOL_WINDOWS):
        c = csum[:, :, g]
        lagged = jnp.pad(c, ((0, 0), (w, 0), (0, 0)))[:, :s]
        count = jnp.minimum(t + 1, w).astype(jnp.float32)[None, :, None]
        outs.append((c - lagged) / count - uf[:, :, g])
    pooled = jnp.stack(outs, axis=2).astype(u.dtype)
    mixed = jnp.einsum('bsgc,gcd->bsgd', pooled, pool_w)
    return mixed.reshape(b, s, POOL_WIDTH) * pool_scale

def _diff_attention(q, k, v, q_gain, k_gain, subln_gain, lam_q1, lam_k1, lam_q2, lam_k2,
                    lambda_init, positions):
    b, s, _ = q.shape
    q = q.reshape(b, s, DIFF_HEADS, 2, HEAD_DIM).transpose(0, 2, 3, 1, 4)
    k = k.reshape(b, s, DIFF_HEADS, 2, HEAD_DIM).transpose(0, 2, 3, 1, 4)
    q = _rope(_rms_norm(q, q_gain), positions)
    k = _rope(_rms_norm(k, k_gain), positions)
    v = _heads(v, DIFF_HEADS)
    lam = (jnp.exp(jnp.sum(lam_q1.astype(jnp.float32) * lam_k1.astype(jnp.float32)))
           - jnp.exp(jnp.sum(lam_q2.astype(jnp.float32) * lam_k2.astype(jnp.float32)))
           + lambda_init)
    scale = HEAD_DIM ** -0.5

    def block(i):
        qb = lax.dynamic_slice_in_dim(q, i * Q_BLOCK, Q_BLOCK, axis=3)
        logits = jnp.einsum('bhmqd,bhmkd->bhmqk', qb, k).astype(jnp.float32) * scale
        qp, kp = _block_positions(i, s)
        probs = jax.nn.softmax(jnp.where(kp <= qp, logits, -jnp.inf), axis=-1)
        weights = probs[:, :, 0] - lam * probs[:, :, 1]
        return jnp.einsum('bhqk,bhkd->bhqd', weights.astype(v.dtype), v)

    o = _sweep_query_blocks(block, s).reshape(b, s, DIFF_HEADS, DIFF_V_DIM)
    o = _rms_norm(o, subln_gain) * (1.0 - lambda_init)
    return o.reshape(b, s, DIFF_WIDTH)

def _stick_breaking_attention(q, k, v):
    b, s, _ = q.shape
    q, k, v = _heads(q, SB_HEADS), _heads(k, SB_HEADS), _heads(v, SB_HEADS)
    scale = HEAD_DIM ** -0.5

    def block(i):
        qb = lax.dynamic_slice_in_dim(q, i * Q_BLOCK, Q_BLOCK, axis=2)
        z = jnp.einsum('bhqd,bhkd->bhqk', qb, k).astype(jnp.float32) * scale
        qp, kp = _block_positions(i, s)
        strict = kp < qp
        log_not_break = jnp.where(strict, jax.nn.log_sigmoid(-z), 0.0)
        later = lax.cumsum(log_not_break, axis=3, reverse=True) - log_not_break
        weights = jnp.where(strict, jnp.exp(jax.nn.log_sigmoid(z) + later), 0.0)
        return jnp.einsum('bhqk,bhkd->bhqd', weights.astype(v.dtype), v)

    return _sweep_query_blocks(block, s)

def _forgetting_attention(q, k, v, f_logit, b_forget, q_gain, k_gain):
    b, s, _ = q.shape
    q = _rms_norm(_heads(q, FOX_HEADS), q_gain)
    k = _rms_norm(_heads(k, FOX_HEADS), k_gain)
    v = _heads(v, FOX_HEADS)
    log_f = jax.nn.log_sigmoid(f_logit.astype(jnp.float32) + b_forget.astype(jnp.float32))
    cum = jnp.cumsum(log_f, axis=1).transpose(0, 2, 1)
    scale = HEAD_DIM ** -0.5

    def block(i):
        qb = lax.dynamic_slice_in_dim(q, i * Q_BLOCK, Q_BLOCK, axis=2)
        cq = lax.dynamic_slice_in_dim(cum, i * Q_BLOCK, Q_BLOCK, axis=2)
        logits = (jnp.einsum('bhqd,bhkd->bhqk', qb, k).astype(jnp.float32) * scale
                  + cq[..., :, None] - cum[..., None, :])
        qp, kp = _block_positions(i, s)
        probs = jax.nn.softmax(jnp.where(kp <= qp, logits, -jnp.inf), axis=-1)
        return jnp.einsum('bhqk,bhkd->bhqd', probs.astype(v.dtype), v)

    return _sweep_query_blocks(block, s)

def _hybrid_mixer(h, w_in, b_gate, b_forget, pool_w, pool_scale, diff_q_norm, diff_k_norm,
                  diff_subln, lam_q1, lam_k1, lam_q2, lam_k2, fox_q_norm, fox_k_norm,
                  w_branch, w_out, lambda_init, positions):
    b, s, _ = h.shape
    proj = jnp.einsum('bsd,dn->bsn', h, w_in)
    offsets = np.cumsum(IN_SPLITS)[:-1].tolist()
    (u_pool, dq, dk, dv, sq, sk, sv, fq, fk, fv, f_logit, g_logit) = jnp.split(proj, offsets, axis=-1)

    o_pool = _pool_mixer(u_pool, pool_w, pool_scale)
    o_diff = _diff_attention(dq, dk, dv, diff_q_norm, diff_k_norm, diff_subln,
                             lam_q1, lam_k1, lam_q2, lam_k2, lambda_init, positions)
    o_sb = _stick_breaking_attention(sq, sk, sv)
    o_fox = _forgetting_attention(fq, fk, fv, f_logit, b_forget, fox_q_norm, fox_k_norm)

    gates = jax.nn.sigmoid(g_logit.reshape(b, s, N_BRANCHES, D_MODEL) + b_gate)
    row_starts = [0] + np.cumsum(BRANCH_WIDTHS)[:-1].tolist()
    merged = jnp.zeros_like(h)
    for n, o in enumerate((o_pool, o_diff, o_sb, o_fox)):
        w_n = w_branch[row_starts[n]:row_starts[n] + BRANCH_WIDTHS[n]]
        merged = merged + gates[:, :, n] * jnp.einsum('bsc,cd->bsd', o, w_n)
    return jnp.einsum('bsd,de->bse', merged, w_out)

def _swiglu(h, w_up, w_down):
    gate, up = jnp.split(jnp.einsum('bsd,df->bsf', h, w_up), 2, axis=-1)
    return jnp.einsum('bsf,fd->bsd', jax.nn.silu(gate) * up, w_down)

def _normal(k, shape, scale):
    return scale * jax.random.normal(k, shape, jnp.float32)

def setup_inputs(seed: int = 0) -> dict:
    key = jax.random.key(seed)
    ks = jax.random.split(key, 22)
    branch_row_scale = jnp.concatenate(
        [jnp.full((w,), w ** -0.5, jnp.float32) for w in BRANCH_WIDTHS])[:, None]
    return {
        'x': _normal(ks[0], (BATCH, SEQ, D_MODEL), 1.0),
        'attn_norm': 1.0 + _normal(ks[1], (DEPTH, D_MODEL), 0.02),
        'ffn_norm': 1.0 + _normal(ks[2], (DEPTH, D_MODEL), 0.02),
        'w_in': _normal(ks[3], (DEPTH, D_MODEL, D_IN), D_MODEL ** -0.5),
        'b_gate': _normal(ks[4], (DEPTH, N_BRANCHES, D_MODEL), 0.1),
        'b_forget': 3.0 + _normal(ks[5], (DEPTH, FOX_HEADS), 0.5),
        'pool_w': _normal(ks[6], (DEPTH, POOL_GROUPS, POOL_GROUP_DIM, POOL_GROUP_DIM), POOL_GROUP_DIM ** -0.5),
        'pool_scale': 1.0 + _normal(ks[7], (DEPTH, POOL_WIDTH), 0.02),
        'diff_q_norm': 1.0 + _normal(ks[8], (DEPTH, HEAD_DIM), 0.02),
        'diff_k_norm': 1.0 + _normal(ks[9], (DEPTH, HEAD_DIM), 0.02),
        'diff_subln': 1.0 + _normal(ks[10], (DEPTH, DIFF_V_DIM), 0.02),
        'lam_q1': _normal(ks[11], (DEPTH, HEAD_DIM), 0.1),
        'lam_k1': _normal(ks[12], (DEPTH, HEAD_DIM), 0.1),
        'lam_q2': _normal(ks[13], (DEPTH, HEAD_DIM), 0.1),
        'lam_k2': _normal(ks[14], (DEPTH, HEAD_DIM), 0.1),
        'fox_q_norm': 1.0 + _normal(ks[15], (DEPTH, HEAD_DIM), 0.02),
        'fox_k_norm': 1.0 + _normal(ks[16], (DEPTH, HEAD_DIM), 0.02),
        'w_branch': _normal(ks[17], (DEPTH, MIX_WIDTH, D_MODEL), 1.0) * branch_row_scale,
        'w_out': _normal(ks[18], (DEPTH, D_MODEL, D_MODEL), D_MODEL ** -0.5),
        'w_ffn_up': _normal(ks[19], (DEPTH, D_MODEL, 2 * D_FF), D_MODEL ** -0.5),
        'w_ffn_down': _normal(ks[20], (DEPTH, D_FF, D_MODEL), D_FF ** -0.5),
    }

def reference(x, attn_norm, ffn_norm, w_in, b_gate, b_forget, pool_w, pool_scale,
              diff_q_norm, diff_k_norm, diff_subln, lam_q1, lam_k1, lam_q2, lam_k2,
              fox_q_norm, fox_k_norm, w_branch, w_out, w_ffn_up, w_ffn_down):
    positions = jnp.arange(x.shape[1], dtype=jnp.int32)
    for layer in range(DEPTH):
        h = _rms_norm(x, attn_norm[layer])
        x = x + _hybrid_mixer(h, w_in[layer], b_gate[layer], b_forget[layer], pool_w[layer],
                              pool_scale[layer], diff_q_norm[layer], diff_k_norm[layer],
                              diff_subln[layer], lam_q1[layer], lam_k1[layer], lam_q2[layer],
                              lam_k2[layer], fox_q_norm[layer], fox_k_norm[layer],
                              w_branch[layer], w_out[layer], _diff_lambda_init(layer), positions)
        h = _rms_norm(x, ffn_norm[layer])
        x = x + _swiglu(h, w_ffn_up[layer], w_ffn_down[layer])
    return x


_drawn_inputs = setup_inputs


def setup_inputs(seed=0):
    import zlib

    import numpy as np

    out = dict(_drawn_inputs(seed))
    spreads = {}
    factors = {'ffn_norm': 3.148,
     'pool_scale': 4.962,
     'diff_q_norm': 5.343,
     'diff_k_norm': 5.142,
     'diff_subln': 5.259,
     'lam_q1': 2.732,
     'lam_q2': 2.81,
     'lam_k2': 2.675,
     'fox_q_norm': 8.0,
     'fox_k_norm': 8.0}
    for name, (base, spread) in spreads.items():
        noise = np.random.default_rng([zlib.crc32(name.encode()), seed]).standard_normal(out[name].shape)
        drawn = base * np.exp(spread * noise) if base else spread * noise
        out[name] = __import__('jax').numpy.asarray(drawn.astype(out[name].dtype))
    for name, factor in factors.items():
        out[name] = (out[name] * factor).astype(out[name].dtype)
    return out
```

```python
import math
from contextlib import ExitStack

import numpy as np

import concourse.bass as bass
from concourse import mybir

F32 = mybir.dt.float32
F32R = mybir.dt.float32r
BF16 = mybir.dt.bfloat16
I32 = mybir.dt.int32
ALU = mybir.AluOpType
ACT = mybir.ActivationFunctionType
AX_X = mybir.AxisListType.X

P = 128
TT = 2
SEQ = TT * P
DEPTH = 2
D = 1024
KD = D // P
HD = 64
NC = 512
D_FF = 2816
KF = D_FF // P
POOL_WINDOWS = (2, 4, 8, 16)
OFF = dict(u=0, dq=256, dk=768, dv=1280, sq=1792, sv=2304, fk=2816, f=3328, gate=3332)
NEG = -1.0e30
EPS = 1e-6
RSQRT_MAGIC = 1597463007.0

ITEMS = [
    ("dq", "w_in", [(OFF["dq"], 512)], KD),
    ("pf", "w_in", [(OFF["u"], 256), (OFF["f"], 4)], KD),
    ("dk", "w_in", [(OFF["dk"], 512)], KD),
    ("ss", "w_in", [(OFF["sq"], 512)], KD),
    ("svfq", "w_in", [(OFF["sv"], 512)], KD),
    ("fkfv", "w_in", [(OFF["fk"], 512)], KD),
    ("dv", "w_in", [(OFF["dv"], 512)], KD),
]
ITEMS += [(("gate", g), "w_in", [(OFF["gate"] + g * NC, NC)], KD) for g in range(8)]
KB = [range(0, 2), range(2, 6), range(6, 8), range(8, 10)]
ITEMS += [(("branch", j, n), "w_branch", [(j * NC, NC)], KB[n]) for j in range(2) for n in range(4)]
ITEMS += [(("out", j), "w_out", [(j * NC, NC)], KD) for j in range(2)]
NPAIR = 5
for _p in range(NPAIR):
    ITEMS += [(("ffg", _p), "w_up", [(_p * NC, NC)], KD), (("ffu", _p), "w_up", [(D_FF + _p * NC, NC)], KD)]
ITEMS += [("fflast", "w_up", [(NPAIR * NC, 256), (D_FF + NPAIR * NC, 256)], KD)]
ITEMS += [(("down", j), "w_down", [(j * NC, NC)], KF) for j in range(2)]
ITEM_AT = {name: n for n, (name, _, _, _) in enumerate(ITEMS)}
NITEM = len(ITEMS)


def item_k(n):
    k = ITEMS[n][3]
    return list(k) if not isinstance(k, int) else list(range(k))


def plan_units():
    units = []
    n = 0
    while n < NITEM:
        name = ITEMS[n][0]
        if name == ("out", 0):
            units += [(n, 0), (n, 2), (n + 1, 0), (n + 1, 2), (n, 4), (n, 6), (n + 1, 4), (n + 1, 6)]
            n += 2
        elif name == ("down", 0):
            for k in range(0, KF - 4, 2):
                units += [(n, k), (n + 1, k)]
            units += [(n, KF - 4), (n, KF - 2), (n + 1, KF - 4), (n + 1, KF - 2)]
            n += 2
        else:
            units += [(n, k) for k in item_k(n)[::2]]
            n += 1
    return units


UNITS = plan_units()
U = len(UNITS)
FIRST = {}
for _u, (_n, _k) in enumerate(UNITS):
    FIRST.setdefault(ITEMS[_n][0], _u)
LAST = {ITEMS[_n][0]: _u for _u, (_n, _k) in enumerate(UNITS)}
GROUPS = {FIRST["dq"]: 4, LAST[("out", 1)] - 3: 4, FIRST[("ffg", 0)]: 4, U - 4: 4}
RAW = 4
RING = 5
AHEAD = 4
assert (OFF["gate"] + 8 * NC, U) == (7428, 144)

G0 = FIRST[("gate", 0)]
B0 = FIRST[("branch", 0, 0)]
O0 = FIRST[("out", 0)]
F0 = FIRST[("ffg", 0)]
JOBS = [("diff", h, G0 + 4 + 3 * h) for h in range(4)] + [("fox", h, G0 + 16 + 3 * h) for h in range(4)]


def timetable(*entries):
    table = {}
    for slot, stage, *args in entries:
        table.setdefault(slot, []).append((stage, *args))
    return table


_PE = [(0, "tr_norm", "attn", 0, 1),
       (10, "tr_qk", "dq"), (10, "cum"), (10, "pool_a"), (12, "pool_b"),
       (18, "tr_ss"), (18, "tr_qk", "dk"),
       (20, "sb_scores", 0), (23, "sb_sums", 0), (25, "sb_out", 0), (25, "tr_fox", "fq"),
       (26, "sb_scores", 1), (29, "sb_sums", 1), (31, "sb_out", 1), (31, "tr_fox", "fk")]
for _kind, _h, _s in JOBS:
    _PE += [(_s, "scores", _kind, _h), (_s + 4, "tr_probs", _kind, _h), (_s + 6, "pv", _kind, _h)]
_PE += [(56, "tr_diff", 0), (57, "tr_diff", 1),
        (B0 + 8, "tr_merged", 0), (O0 + 2, "tr_merged", 1),
        (F0, "tr_norm", "ffn", 0, 1)]
for _p in range(NPAIR):
    _PE += [(FIRST[("ffu", _p)] + 6, "tr_act", _p)]
_PE += [(LAST["fflast"] + 3, "tr_act", NPAIR)]
_PE.sort(key=lambda e: e[0])
PE_TIMETABLE = timetable(*_PE)
BIAS_AT = [G0 + 1 + 4 * g for g in range(8)]
PE_MID = {0: [("tr_norm", "attn", 1, 0), ("tr_norm", "attn", 1, 1)],
          F0 - 4: [("tr_norm", "ffn", 0, 0)],
          F0: [("tr_norm", "ffn", 1, 0), ("tr_norm", "ffn", 1, 1)]}
PE_NEXT = ("tr_norm", "attn", 0, 0)

def stage_parts(stage, *args):
    if stage == "tr_norm":
        which, t, b = args
        return [((stage, which, t, b), "ABTO"[2 * t + b])]
    if stage == "tr_qk":
        return [((stage, args[0], t), "AB"[t]) for t in range(TT)]
    if stage == "tr_fox":
        return [((stage, args[0], t), "AB"[t]) for t in range(TT)]
    if stage == "tr_ss":
        return [((stage, t), "TO"[t]) for t in range(TT)]
    if stage in ("cum", "pool_b"):
        return [((stage,), "T")]
    if stage == "pool_a":
        return [((stage,), "O")]
    if stage in ("sb_scores", "sb_sums"):
        return [((stage, args[0]), "AB")]
    if stage == "sb_out":
        return [((stage, args[0]), "O")]
    if stage == "scores":
        kind, h = args
        return [((stage, kind, h), "AB" if kind == "diff" else "AB"[h % 2])]
    if stage == "tr_probs":
        return [((stage, *args), "T")]
    if stage == "pv":
        return [((stage, *args), "O")]
    if stage == "tr_diff":
        return [((stage, args[0]), "TO"[args[0]])]
    if stage == "tr_merged":
        return [((stage, args[0], t), ("AB", "TO")[args[0]][t]) for t in range(TT)]
    if stage == "tr_act":
        return [((stage, args[0], t), ("AB", "TO")[args[0] % 2][t]) for t in range(TT)]
    raise ValueError(stage)


STAGE_EVENTS = [e for e, _ in stage_parts(*PE_NEXT)]
for _u in range(U):
    for _s in PE_TIMETABLE.get(_u, []) + PE_MID.get(_u, []):
        STAGE_EVENTS += [e for e, _ in stage_parts(*_s)]


EARLY = [name for g, size in GROUPS.items() for name, last in LAST.items() if g <= last < g + size]


_SV = [(0, "norm_evac", "attn", 0, 0), (0, "norm_evac", "attn", 0, 1), (0, "squares", "attn", 0), (0, "residual", "down", 1, 1), (0, "gain", "attn", 1, 1),
       (1, "norm_evac", "attn", 1, 0), (1, "norm_evac", "attn", 1, 1), (1, "squares", "attn", 1),
       (4, "qk_norm", "dq"), (8, "pf"), (8, "fox_forget"), (10, "qk_evac", "dq"), (10, "cum_evac"),
       (10, "pool_evac_a"), (12, "pool_evac_b"),
       (12, "qk_norm", "dk"), (16, "ss"), (18, "ss_evac"), (18, "qk_evac", "dk"),
       (20, "svfq"), (20, "sb_logs", 0), (23, "sb_weights", 0), (24, "fkfv"), (25, "sb_evac", 0),
       (25, "fox_evac", "fq"), (26, "sb_logs", 1), (28, "dv"), (29, "sb_weights", 1),
       (31, "sb_evac", 1), (31, "fox_evac", "fk")]
for _kind, _h, _s in JOBS:
    _SV += [(_s, "maxima", _kind, _h), (_s + 1, "softmax", _kind, _h), (_s + 4, "probs_evac", _kind, _h),
            (_s + 6, "pv_evac", _kind, _h)]
_SV += [(51, "diff_norm"), (56, "diff_evac", 0), (57, "diff_evac", 1)]
for _g in range(8):
    _SV += [(FIRST[("gate", _g)] + 4, "gate", _g)]
_SV += [(57, "sigmoid", 0), (58, "sigmoid", 1), (59, "sigmoid", 2), (60, "sigmoid", 3)]
for _j in range(2):
    for _n in range(4):
        _SV += [(LAST[("branch", _j, _n)] + 1, "branch", _j, _n)]
_SV += [(B0 + 8, "merged_evac", 0), (O0 + 2, "merged_evac", 1),
        (F0 - 3, "residual", "out", 0, 0), (F0 - 3, "gain", "ffn", 0, 0),
        (F0 - 3, "residual", "out", 0, 1), (F0 - 3, "gain", "ffn", 0, 1),
        (F0 - 1, "residual", "out", 1, 0), (F0 - 1, "gain", "ffn", 1, 0),
        (F0, "norm_evac", "ffn", 0, 0), (F0, "norm_evac", "ffn", 0, 1), (F0, "squares", "ffn", 0), (F0, "residual", "out", 1, 1), (F0, "gain", "ffn", 1, 1),
        (F0 + 1, "norm_evac", "ffn", 1, 0), (F0 + 1, "norm_evac", "ffn", 1, 1), (F0 + 1, "squares", "ffn", 1), (F0 + 2, "norm_ffn")]
for _p in range(NPAIR):
    _SV += [(FIRST[("ffu", _p)], "ff_gate", _p), (FIRST[("ffu", _p)] + 4, "ff_up", _p),
            (FIRST[("ffu", _p)] + 6, "act_evac", _p)]
_SV += [(LAST["fflast"] + 1, "ff_gate", NPAIR), (LAST["fflast"] + 1, "ff_up", NPAIR),
        (LAST["fflast"] + 3, "act_evac", NPAIR),
        (U - 3, "residual", "down", 0, 0), (U - 3, "gain", "attn", 0, 0),
        (U - 3, "residual", "down", 0, 1), (U - 3, "gain", "attn", 0, 1),
        (U - 1, "residual", "down", 1, 0), (U - 1, "gain", "attn", 1, 0)]
_SV.sort(key=lambda e: e[0])
SV_TIMETABLE = timetable(*_SV)
_ORDER = [tuple(e[1:]) for e in _SV]


def order(stage, spread=lambda *a: [a]):
    return [e for s in _ORDER if s[0] == stage for e in spread(*s[1:])]


def evac_events():
    out = []
    for s in _ORDER:
        if s[0] == "norm_evac":
            out += [("norm", *s[1:])]
        elif s[0] == "pool_evac_b":
            out += [("pool", 0), ("pool", 1)]
        elif s[0] == "sb_evac":
            out += [("sb", s[1])]
        elif s[0] == "pv_evac" and s[1] == "fox":
            out += [("fox", s[2])]
        elif s[0] == "diff_evac":
            out += [("diff", s[1])]
        elif s[0] == "merged_evac":
            out += [("merged", s[1], t) for t in range(TT)]
        elif s[0] == "act_evac":
            out += [("act", s[1], t) for t in range(TT)]
    return out


def constant_blocks():
    q = np.arange(P)
    key, col = q[:, None], q[None, :]
    blocks = {}
    blocks["ident"] = np.eye(P)
    blocks["causal"] = np.where(col > key, NEG, 0.0)
    blocks["strict_neg"] = np.where(key >= col, NEG, 0.0)
    blocks["strict"] = (key < col) * 1.0
    blocks["upto"] = (key <= col) * 1.0
    blocks["ones"] = np.ones((P, P))
    blocks["minus_from"] = (key >= col) * -1.0
    blocks["minus_ones"] = -np.ones((P, P))
    half = HD // 2
    inv = np.float32(10000.0) ** (-np.arange(half, dtype=np.float32) / np.float32(half))
    ang = np.arange(SEQ, dtype=np.float32)[:, None] * inv[None, :]
    cos, sin = np.cos(ang), np.sin(ang)
    cc = np.concatenate([cos, cos], 1).reshape(TT, P, HD)
    ss = np.concatenate([-sin, sin], 1).reshape(TT, P, HD)
    blocks["cos"] = cc.transpose(1, 0, 2).reshape(P, -1)
    blocks["sin"] = ss.transpose(1, 0, 2).reshape(P, -1)
    src, dst = np.arange(SEQ)[:, None], np.arange(SEQ)[None, :]
    for g, w in enumerate(POOL_WINDOWS):
        band = ((src <= dst) & (src > dst - w)) / np.minimum(dst + 1, w) - (src == dst)
        blocks[f"band0_{g}"] = band[0:P, :]
        blocks[f"band1_{g}"] = band[P:, P:]
    lam = [0.8 - 0.6 * math.exp(-0.3 * layer) for layer in range(DEPTH)]
    blocks["lam"] = np.tile(np.array(lam), (P, 1))
    blocks["one_minus_lam"] = np.tile(1.0 - np.array(lam), (P, 1))
    return {n: np.ascontiguousarray(b, dtype=np.float32) for n, b in blocks.items()}


def build(nc, x, attn_norm, ffn_norm, w_in, b_gate, b_forget, pool_w, pool_scale, diff_q_norm,
          diff_k_norm, diff_subln, lam_q1, lam_k1, lam_q2, lam_k2, fox_q_norm, fox_k_norm,
          w_branch, w_out, w_ffn_up, w_ffn_down, consts, out):
    cblocks = constant_blocks()
    ccol, ncol = {}, 0
    for name, block in cblocks.items():
        ccol[name] = (ncol, block.shape[1])
        ncol += block.shape[1]
    weights = {"w_in": w_in, "w_branch": w_branch, "w_out": w_out, "w_up": w_ffn_up, "w_down": w_ffn_down}

    with ExitStack() as ctx:
        def sb(name, shape, dt=F32, stack=ctx):
            return stack.enter_context(nc.sbuf_tensor(name, shape, dt))

        event_order = {}

        def signal(name, events):
            events = list(events)
            semaphore = ctx.enter_context(nc.semaphore(name))
            event_order[id(semaphore)] = {e: i + 1 for i, e in enumerate(events)}
            assert len(event_order[id(semaphore)]) == len(events)
            return semaphore

        def nth(semaphore, layer, event):
            order_in_layer = event_order[id(semaphore)]
            return layer * len(order_in_layer) + order_in_layer[event]

        def sem(name):
            return ctx.enter_context(nc.semaphore(name))

        raw = sb("raw", [P, RAW, 2, NC])
        w_hi = sb("w_hi", [P, RING, 2, NC], F32R)
        w_lo = sb("w_lo", [P, RING, 2, NC], F32R)
        x_sb = sb("x_sb", [P, TT, D])
        hT = [sb("hT_hi", [P, KD, SEQ], F32R), sb("hT_lo", [P, KD, SEQ], F32R)]
        wide = sb("wide", [P, TT, 4 * D])
        con = sb("con", [P, ncol])
        masks = sb("masks", [P, 3, P], BF16)
        bias = sb("bias", [P, 2, NC])
        gains = sb("gains", [P, 4, HD])
        ropeA = sb("ropeA", [P, 2, TT, HD])
        ropeB = sb("ropeB", [P, 2, TT, HD])
        lamv = sb("lamv", [P, 4, HD])
        poolw = sb("poolw", [P, 2, P])
        small = sb("small", [P, 16])
        b_f, psc, subln = small[:, 0:4], small[:, 4:6], small[:, 6:7]
        gsub, neglam, lam_e, lam_s = small[:, 7:8], small[:, 8:9], small[:, 9:11], small[:, 11:13]
        stat = sb("stat", [P, 80])
        eps_heads = sb("eps_heads", [P, TT])
        row_max = sb("row_max", [P, 4])
        inverse = sb("inverse", [P, 4])
        y_norm = {"attn": sb("y_attn", [P, TT]), "ffn": sb("y_ffn", [P, TT])}
        ssq = sb("ssq", [P, TT, 2])
        nmx = sb("nmx", [P, 4])
        den = sb("den", [P, 4])
        fg = sb("fg", [P, 5, 8])
        mixing = ExitStack()
        oT = [sb("oT_hi", [P, 10, SEQ], F32R, mixing), sb("oT_lo", [P, 10, SEQ], F32R, mixing)]
        qT = {"dq": sb("dqT", [P, 4, SEQ], F32, mixing), "dk": sb("dkT", [P, 4, SEQ], F32, mixing),
              "fq": sb("fqT", [HD + 2, 4, SEQ], F32, mixing), "fk": sb("fkT", [HD + 2, 4, SEQ], F32, mixing)}
        sT = sb("sT", [P, 4, SEQ], F32, mixing)
        v_d = sb("v_d", [P, TT, 512], F32, mixing)
        v_s = sb("v_s", [P, TT, 256], F32, mixing)
        v_f = sb("v_f", [P, TT, 256], F32, mixing)
        aug = {"fq": sb("q_aug", [P, TT, 4, HD + 2], F32, mixing), "fk": sb("k_aug", [P, TT, 4, HD + 2], F32, mixing)}
        sb1 = sb("sb1", [P, 2, 384], F32, mixing)
        sb2 = sb("sb2", [P, 2, 384], F32, mixing)
        expd = sb("expd", [P, 2, 384], F32, mixing)
        probs = sb("probs", [P, 384], F32, mixing)
        probsT = sb("probsT", [P, 384], F32, mixing)
        o_d = sb("o_d", [P, TT, 4, P], F32, mixing)
        mixing.close()
        ffn_area = ExitStack()
        aT = [sb("aT_hi", [P, KF, SEQ], F32R, ffn_area), sb("aT_lo", [P, KF, SEQ], F32R, ffn_area)]
        ffn_area.close()

        def scratch(t, n, width=512):
            return wide[:, t, 2048 + n * 512:2048 + n * 512 + width]
        XN, TA, TB, SQ = range(4)
        pool_u = [wide[:, t, 1024:1280] for t in range(TT)]
        pooledT = wide[:, 0, 1536:2048]

        def hn(t):
            return wide[:, t, 0:D]
        gain_row = {"ffn": wide[:, 0, D:2 * D], "attn": wide[:, 1, D:2 * D]}

        def merged(t):
            return wide[:, t, 0:D]

        def ff_tmp(t, p, width):
            return wide[:, t, 2048 + 1024 * (p % 2):2048 + 1024 * (p % 2) + width]

        def ff_act(t, p, width):
            return wide[:, t, 2560 + 1024 * (p % 2):2560 + 1024 * (p % 2) + width]

        def c(name):
            a, w = ccol[name]
            return con[:, a:a + w]

        bulk = ctx.enter_context(nc.psum_tensor("bulk", [P, 2, TT, NC], F32))
        bankAB = ctx.enter_context(nc.psum_tensor("bankAB", [P, 2, NC], F32))
        bankT = ctx.enter_context(nc.psum_tensor("bankT", [P, NC], F32))
        bankO = ctx.enter_context(nc.psum_tensor("bankO", [P, NC], F32))
        bank = {"A": bankAB[:, 0, :], "B": bankAB[:, 1, :], "T": bankT[:, :], "O": bankO[:, :]}

        y_attn, y_ffn = y_norm["attn"], y_norm["ffn"]

        def item_bank(layer, n, t):
            return bulk[:, (layer * NITEM + n) % 2, t, :]

        raw_loaded = [sem(f"raw_loaded{s}") for s in range(RAW)]
        hi_ready = signal("hi_ready", range(U))
        lo_ready = signal("lo_ready", range(U))
        unit_done = signal("unit_done", range(U))
        early_done = signal("early_done", EARLY)
        stage_done = signal("stage_done", STAGE_EVENTS)
        evacs = evac_events()
        lhs_hi = signal("lhs_hi", evacs)
        lhs_lo = signal("lhs_lo", evacs)
        identity_loaded, consts_loaded, params_loaded = sem("identity_loaded"), sem("consts_loaded"), sem("params_loaded")
        x_loaded = [sem("x_loaded0"), sem("x_loaded1")]
        gain_loaded = {"attn": sem("attn_gain_loaded"), "ffn": sem("ffn_gain_loaded")}
        bias_loaded = [sem("bias_loaded0"), sem("bias_loaded1")]
        stored = sem("stored")
        masks_ready, fills_ready = sem("masks_ready"), sem("fills_ready")
        act_step, vec_step, pool_step = sem("act_step"), sem("vec_step"), sem("pool_step")
        squares = signal("squares", [(w, t) for w in ("dq", "dk", "fq", "fk") for t in range(TT)])
        normed = signal("normed", [(w, t) for w in ("dq", "dk", "fq", "fk") for t in range(TT)])
        rotated = signal("rotated", [(w, t) for w in ("dq", "dk", "fq", "fk") for t in range(TT)])
        tables_ready = signal("tables_ready", ["rope"])
        u_ready = signal("u_ready", range(TT))
        forget_in = signal("forget_in", range(TT))
        forget_ln = signal("forget_ln", ["ln"])
        forget_out = signal("forget_out", ["softplus", "aug"])
        pooled = signal("pooled", ["pooled"])
        qkT_ready = signal("qkT_ready", [(w, t) for w in ("dq", "dk", "fq", "fk") for t in range(TT)])
        ss_staged = signal("ss_staged", range(TT))
        sT_ready = signal("sT_ready", range(TT))
        sb_ln = signal("sb_ln", range(2))
        sb_sp = signal("sb_sp", range(2))
        sb_w = signal("sb_w", range(2))
        v_ready = signal("v_ready", [(v, t) for v in ("sv", "fv", "dv") for t in range(TT)])
        jobs = [(k, h) for k, h, _ in JOBS]
        maxed = signal("maxed", jobs)
        exped = signal("exped", jobs)
        probs_ready = signal("probs_ready", jobs)
        probsT_ready = signal("probsT_ready", jobs)
        o_d_ready = signal("o_d_ready", range(4))
        o_sq = signal("o_sq", ["squares"])
        o_normed = signal("o_normed", ["normed"])
        lam_exp = signal("lam_exp", ["exp"])
        lam_sum = signal("lam_sum", ["sum", "lam"])
        gate_ready = signal("gate_ready", [(g, t) for g in range(8) for t in range(TT)])
        gate_open = signal("gate_open", [(n, t) for n in range(4) for t in range(TT)])
        gated = signal("gated", [(j, n, t) for j in range(2) for n in range(4) for t in range(TT)])
        summed = signal("summed", [(j, n) for j in range(2) for n in (1, 2)])
        merged_ready = signal("merged_ready", [(j, t) for j in range(2) for t in range(TT)])
        x_out = signal("x_out", [(t, j) for t in range(TT) for j in range(2)])
        x_down = signal("x_down", [(t, j) for t in range(TT) for j in range(2)])
        sumsq = {w: signal(f"sumsq_{w}", [(t, j) for t in range(TT) for j in range(2)]) for w in ("attn", "ffn")}
        hn_ready = {w: signal(f"hn_ready_{w}", [(t, j) for t in range(TT) for j in range(2)]) for w in ("attn", "ffn")}
        y_ready = {w: signal(f"y_ready_{w}", ["y"]) for w in ("attn", "ffn")}
        ff_sig = signal("ff_sig", [(p, t) for p in range(NPAIR + 1) for t in range(TT)])
        ff_gated = signal("ff_gated", [(p, t) for p in range(NPAIR + 1) for t in range(TT)])
        ff_ready = signal("ff_ready", [(p, t) for p in range(NPAIR + 1) for t in range(TT)])

        def wait_item(engine, layer, name, t):
            if t == 0 and name in EARLY:
                engine.wait_ge(early_done, nth(early_done, layer, name))
            else:
                engine.wait_ge(unit_done, nth(unit_done, layer, LAST[name]))

        def released_by(name, t):
            return {
                "dq": (normed, ("dq", t)), "pf": (u_ready, t), "dk": (normed, ("dk", t)), "ss": (ss_staged, t),
                "svfq": (normed, ("fq", t)), "fkfv": (normed, ("fk", t)), "dv": (v_ready, ("dv", t)),
                "gate": (gate_ready, (name[1], t)), "branch": (gated, (*name[1:], t)),
                "out": (x_out, (t, name[1])), "down": (x_down, (t, name[1])),
                "ffg": (ff_gated, (name[1], t)), "ffu": (ff_ready, (name[1], t)), "fflast": (ff_ready, (NPAIR, t)),
            }[name if isinstance(name, str) else name[0]]

        PARAM_DMAS = 16

        block = ctx.enter_context(nc.Block())

        @block.sync
        def _(sp):
            filled = [0] * RAW

            def load_unit(g):
                layer, u = divmod(g, U)
                n, k = UNITS[u]
                name, matrix, columns, _ = ITEMS[n]
                if g >= RAW:
                    sp.wait_ge(lo_ready, nth(lo_ready, *divmod(g - RAW, U)))
                rows = weights[matrix][layer, k * P:(k + 2) * P, :].rearrange("(k p) n -> p k n", p=P)
                at = 0
                for c0, w in columns:
                    sp.dma_start(raw[:, g % RAW, :, at:at + w], rows[:, :, c0:c0 + w]).then_inc(raw_loaded[g % RAW], 16)
                    at += w
                    filled[g % RAW] += 16

            def load_param(layer, n):
                if layer and n == 0:
                    sp.wait_ge(gated, nth(gated, layer - 1, (1, 3, 1)))
                if n < 4:
                    g = (diff_q_norm, diff_k_norm, fox_q_norm, fox_k_norm)[n]
                    dst, src = gains[:, n, :], g[layer].partition_broadcast(P)
                elif n < 8:
                    g = (lam_q1, lam_k1, lam_q2, lam_k2)[n - 4]
                    dst, src = lamv[:, n - 4, :], g[layer].partition_broadcast(P)
                elif n < 12:
                    g, r = n - 8, (n % 2) * HD
                    dst, src = poolw[r:r + HD, g // 2, r:r + HD], pool_w[layer, g]
                elif n < 14:
                    i = n - 12
                    dst, src = psc[:, i:i + 1], pool_scale[layer, i * P:(i + 1) * P].rearrange("(p c) -> p c", c=1)
                elif n == 14:
                    dst, src = b_f, b_forget[layer].partition_broadcast(P)
                else:
                    dst, src = subln, diff_subln[layer].rearrange("(p c) -> p c", c=1)
                sp.dma_start(dst, src).then_inc(params_loaded, 16)

            sp.dma_start(x_sb[:, 0, :], x[0, 0:P, :]).then_inc(x_loaded[0], 16)
            sp.dma_start(gain_row["attn"], attn_norm[0].partition_broadcast(P)).then_inc(gain_loaded["attn"], 16)
            sp.dma_start(con[:, 0:P], consts[:, 0:P]).then_inc(identity_loaded, 16)
            for g in range(RAW):
                if g == 2:
                    sp.dma_start(x_sb[:, 1, :], x[0, P:SEQ, :]).then_inc(x_loaded[1], 16)
                load_unit(g)
            sp.dma_start(con[:, P:ncol], consts[:, P:ncol]).then_inc(consts_loaded, 16)
            sp.wait_ge(fills_ready, 1)
            for n in range(PARAM_DMAS):
                load_param(0, n)
            for layer in range(DEPTH):
                for u in range(U):
                    if u in BIAS_AT:
                        g = BIAS_AT.index(u)
                        if g >= 2:
                            sp.wait_ge(gate_ready, nth(gate_ready, layer, (g - 2, 1)))
                        elif layer:
                            sp.wait_ge(gate_ready, nth(gate_ready, layer - 1, (6 + g, 1)))
                        sp.dma_start(bias[:, g % 2, :], b_gate[layer, g // 2, (g % 2) * NC:(g % 2 + 1) * NC]
                                     .partition_broadcast(P)).then_inc(bias_loaded[g % 2], 16)
                    if u == O0 + 5:
                        sp.wait_ge(summed, nth(summed, layer, (1, 1)))
                        sp.dma_start(gain_row["ffn"], ffn_norm[layer].partition_broadcast(P)).then_inc(gain_loaded["ffn"], 16)
                        if layer + 1 < DEPTH:
                            sp.dma_start(gain_row["attn"], attn_norm[layer + 1].partition_broadcast(P)).then_inc(gain_loaded["attn"], 16)
                    if layer + 1 < DEPTH and F0 + 8 <= u < F0 + 8 + PARAM_DMAS:
                        load_param(layer + 1, u - F0 - 8)
                    if layer * U + u + RAW < DEPTH * U:
                        load_unit(layer * U + u + RAW)
            for t in range(TT):
                sp.wait_ge(x_down, nth(x_down, DEPTH - 1, (t, 1)))
                sp.dma_start(out[0, t * P:(t + 1) * P, :], x_sb[:, t, :]).then_inc(stored, 16)
            sp.wait_ge(stored, 32)

        @block.gpsimd
        def _(pool):
            steps = [0]

            def count_step():
                steps[0] += 1
                return steps[0]

            pool.memset(poolw[:, :, :], 0.0).then_inc(pool_step, 1)
            pool.wait_ge(pool_step, count_step())
            pool.memset(aug["fq"][:, :, :, HD:HD + 1], 1.0).then_inc(pool_step, 1)
            pool.wait_ge(pool_step, count_step())
            pool.memset(aug["fk"][:, :, :, HD + 1:HD + 2], 1.0).then_inc(fills_ready, 1)
            pool.wait_ge(consts_loaded, 16)
            cos = c("cos").rearrange("p (t d) -> p t d", t=TT)
            sin = c("sin").rearrange("p (t d) -> p t d", t=TT)
            half = HD // 2
            for layer in range(DEPTH):
                pool.wait_ge(params_loaded, 16 * PARAM_DMAS * (layer + 1))
                for i in range(2):
                    g = gains[:, i:i + 1, :].broadcast_to([P, TT, HD])
                    pool.tensor_tensor(ropeA[:, i, :, :], cos, g, ALU.mult)
                    pool.tensor_tensor(ropeB[:, i, :, 0:half], sin[:, :, 0:half], g[:, :, half:HD], ALU.mult)
                    last = pool.tensor_tensor(ropeB[:, i, :, half:HD], sin[:, :, half:HD], g[:, :, 0:half], ALU.mult)
                last = pool.tensor_scalar(gains[:, 2, :], gains[:, 2, :], HD ** -0.5, None, ALU.mult)
                last.then_inc(tables_ready, 1)
                pool.wait_ge(tables_ready, nth(tables_ready, layer, "rope"))

                def rotate(which, t):
                    i = ("dq", "dk").index(which)
                    pool.wait_ge(normed, nth(normed, layer, (which, t)))
                    xn = scratch(t, XN).rearrange("p (h d) -> p h d", d=HD)
                    ta = scratch(t, TA).rearrange("p (h d) -> p h d", d=HD)
                    tb = scratch(t, TB).rearrange("p (h d) -> p h d", d=HD)
                    pool.tensor_tensor(ta, xn, ropeA[:, i, t:t + 1, :].broadcast_to([P, 8, HD]), ALU.mult)
                    pool.tensor_tensor(tb[:, :, 0:half], xn[:, :, half:HD],
                                       ropeB[:, i, t:t + 1, 0:half].broadcast_to([P, 8, half]), ALU.mult)
                    pool.tensor_tensor(tb[:, :, half:HD], xn[:, :, 0:half],
                                       ropeB[:, i, t:t + 1, half:HD].broadcast_to([P, 8, half]), ALU.mult).then_inc(pool_step, 1)
                    pool.wait_ge(pool_step, count_step())
                    pool.tensor_tensor(xn, ta, tb, ALU.add).then_inc(rotated, 1)

                def fox_gain(which, t):
                    i = 2 + ("fq", "fk").index(which)
                    pool.wait_ge(normed, nth(normed, layer, (which, t)))
                    pool.tensor_tensor(
                        aug[which][:, t, :, 0:HD], scratch(t, XN, 256).rearrange("p (h d) -> p h d", d=HD),
                        gains[:, i:i + 1, :].broadcast_to([P, 4, HD]), ALU.mult).then_inc(rotated, 1)

                for which in ("dq", "dk"):
                    for t in range(TT):
                        rotate(which, t)
                for which in ("fq", "fk"):
                    for t in range(TT):
                        fox_gain(which, t)
                pool.wait_ge(o_d_ready, nth(o_d_ready, layer, 3))
                for t in range(TT):
                    last = pool.tensor_tensor(scratch(t, TB).rearrange("p (h d) -> p h d", h=4),
                                              o_d[:, t, :, :], o_d[:, t, :, :], ALU.mult)
                last.then_inc(o_sq, 1)
                for j in range(2):
                    for n in range(1, 4):
                        for t in range(TT):
                            pool.wait_ge(gated, nth(gated, layer, (j, n, t)))
                            m = merged(t)[:, j * NC:(j + 1) * NC]
                            ins = pool.tensor_tensor(m, m, wide[:, t, n * D + j * NC:n * D + (j + 1) * NC], ALU.add)
                            if n == 3:
                                ins.then_inc(merged_ready, 1)
                            elif t == 1:
                                ins.then_inc(summed, 1)
                                pool.wait_ge(summed, nth(summed, layer, (j, n)))

        @block.scalar
        def _(act):
            steps = [0]

            def count_step():
                steps[0] += 1
                return steps[0]

            loaded = [0] * RAW

            def split_hi(g):
                layer, u = divmod(g, U)
                width = sum(w for _, w in ITEMS[UNITS[u][0]][2])
                loaded[g % RAW] += 16 * len(ITEMS[UNITS[u][0]][2])
                act.wait_ge(raw_loaded[g % RAW], loaded[g % RAW])
                if g >= RING:
                    act.wait_ge(unit_done, nth(unit_done, *divmod(g - RING, U)))
                act.activation(w_hi[:, g % RING, :, 0:width], raw[:, g % RAW, :, 0:width], ACT.Copy).then_inc(hi_ready, 1)

            def lhs_part(layer, event, dst, src, scale=None):
                ins = act.activation(dst, src, ACT.Copy) if scale is None else act.activation(dst, src, ACT.Copy, scale=scale)
                ins.then_inc(lhs_hi, 1)

            def row_squares(layer, which, t):
                for j in range(2):
                    if which == "ffn":
                        act.wait_ge(x_out, nth(x_out, layer, (t, j)))
                    elif layer:
                        act.wait_ge(x_down, nth(x_down, layer - 1, (t, j)))
                    elif j == 0:
                        act.wait_ge(x_loaded[t], 16)
                    act.activation(scratch(t, 2 + j), x_sb[:, t, j * NC:(j + 1) * NC],
                                   ACT.Square, accum_out=ssq[:, t, j:j + 1]).then_inc(sumsq[which], 1)

            def norm_evac(layer, which, t, b):
                act.wait_ge(stage_done, nth(stage_done, layer, ("tr_norm", which, t, b)))
                lhs_part(layer, ("norm", which, t, b), hT[0][:, 4 * b:4 * b + 4, t * P:(t + 1) * P],
                         bank["ABTO"[2 * t + b]].rearrange("p (k q) -> p k q", k=4))

            def head_squares(layer, which, item, c0, width, copy_to=None):
                for t in range(TT):
                    wait_item(act, layer, item, t)
                    src = item_bank(layer, ITEM_AT[item], t)
                    if copy_to is not None:
                        act.activation(copy_to[:, t, :], src[:, 256 - c0:512 - c0], ACT.Copy, scale=y_attn[:, t:t + 1]).then_inc(v_ready, 1)
                    act.activation(scratch(t, SQ, width), src[:, c0:c0 + width], ACT.Square).then_inc(squares, 1)

            def qk_norm(layer, which):
                if which == "dk":
                    act.wait_ge(normed, nth(normed, layer, ("dq", 1)))
                else:
                    act.wait_ge(sumsq["attn"], nth(sumsq["attn"], layer, (1, 1)))
                head_squares(layer, which, which, 0, 512)

            def fox_forget(layer):
                act.wait_ge(forget_in, nth(forget_in, layer, 1))
                v, a, e, l = (fg[:, i, :] for i in range(4))
                act.activation(a, v, ACT.Abs).then_inc(act_step, 1)
                act.wait_ge(act_step, count_step())
                act.activation(e, a, ACT.Exp, scale=-1.0).then_inc(act_step, 1)
                act.wait_ge(act_step, count_step())
                act.activation(l, e, ACT.Ln, bias=1.0).then_inc(forget_ln, 1)
                act.wait_ge(lam_sum, nth(lam_sum, layer, "sum"))
                act.activation(lam_e, lam_s, ACT.Exp).then_inc(lam_exp, 1)

            def qk_evac(layer, which):
                for t in range(TT):
                    act.wait_ge(stage_done, nth(stage_done, layer, ("tr_qk", which, t)))
                    act.activation(
                        qT[which][:, :, t * P:(t + 1) * P], bank["AB"[t]].rearrange("p (h q) -> p h q", h=4),
                        ACT.Copy, scale=HD ** -0.5 if which == "dq" else 1.0).then_inc(qkT_ready, 1)

            def pool_evac_a(layer):
                act.wait_ge(stage_done, nth(stage_done, layer, ("pool_a",)))
                act.activation(pooledT, bank["O"], ACT.Copy).then_inc(pooled, 1)

            def pool_evac_b(layer):
                act.wait_ge(stage_done, nth(stage_done, layer, ("pool_b",)))
                for pr in range(2):
                    lhs_part(layer, ("pool", pr), oT[0][:, pr, :], bank["T"][:, pr * SEQ:(pr + 1) * SEQ], psc[:, pr:pr + 1])

            def ss(layer):
                act.wait_ge(normed, nth(normed, layer, ("dk", 1)))
                for t in range(TT):
                    wait_item(act, layer, "ss", t)
                    src = item_bank(layer, ITEM_AT["ss"], t)
                    act.activation(scratch(t, SQ), src, ACT.Copy, scale=y_attn[:, t:t + 1]).then_inc(ss_staged, 1)

            def ss_evac(layer):
                for t in range(TT):
                    act.wait_ge(stage_done, nth(stage_done, layer, ("tr_ss", t)))
                    src = bank["TO"[t]].rearrange("p (k q) -> p k q", k=4)
                    act.activation(sT[:, 0:2, t * P:(t + 1) * P], src[:, 0:2, :], ACT.Copy, scale=HD ** -0.5)
                    act.activation(sT[:, 2:4, t * P:(t + 1) * P], src[:, 2:4, :], ACT.Copy).then_inc(sT_ready, 1)

            def dv(layer):
                for t in range(TT):
                    wait_item(act, layer, "dv", t)
                    act.activation(v_d[:, t, :], item_bank(layer, ITEM_AT["dv"], t), ACT.Copy, scale=y_attn[:, t:t + 1]).then_inc(v_ready, 1)

            def pf(layer):
                act.wait_ge(y_ready["attn"], nth(y_ready["attn"], layer, "y"))
                for t in range(TT):
                    act.wait_ge(forget_in, nth(forget_in, layer, t))
                    act.activation(pool_u[t], item_bank(layer, ITEM_AT["pf"], t)[:, 0:256], ACT.Copy,
                                   scale=y_attn[:, t:t + 1]).then_inc(u_ready, 1)

            def sb_logs(layer, pair):
                act.wait_ge(stage_done, nth(stage_done, layer, ("sb_scores", pair)))
                act.activation(sb1[:, :, :], bankAB[:, :, 0:384], ACT.Abs).then_inc(act_step, 1)
                act.wait_ge(act_step, count_step())
                act.activation(sb2[:, :, :], sb1[:, :, :], ACT.Exp, scale=-1.0).then_inc(act_step, 1)
                act.wait_ge(act_step, count_step())
                act.activation(sb1[:, :, :], sb2[:, :, :], ACT.Ln, bias=1.0).then_inc(sb_ln, 1)

            def sb_weights(layer, pair):
                act.wait_ge(stage_done, nth(stage_done, layer, ("sb_sums", pair)))
                act.activation(sb1[:, :, :], bankAB[:, :, 0:384], ACT.Exp).then_inc(sb_w, 1)

            def sb_evac(layer, pair):
                act.wait_ge(stage_done, nth(stage_done, layer, ("sb_out", pair)))
                lhs_part(layer, ("sb", pair), oT[0][:, 6 + pair, :], bank["O"][:, 0:SEQ])

            def svfq(layer):
                for t in range(TT):
                    act.wait_ge(stage_done, nth(stage_done, layer, ("tr_ss", t)))
                head_squares(layer, "fq", "svfq", 256, 256, v_s)

            def fkfv(layer):
                act.wait_ge(normed, nth(normed, layer, ("fq", 1)))
                head_squares(layer, "fk", "fkfv", 0, 256, v_f)

            def fox_evac(layer, which):
                for t in range(TT):
                    act.wait_ge(stage_done, nth(stage_done, layer, ("tr_fox", which, t)))
                    act.activation(
                        qT[which][:, :, t * P:(t + 1) * P], bank["AB"[t]][0:HD + 2, :].rearrange("p (h q) -> p h q", h=4),
                        ACT.Copy).then_inc(qkT_ready, 1)

            def softmax(layer, kind, h):
                act.wait_ge(maxed, nth(maxed, layer, (kind, h)))
                if (kind, h) != jobs[0]:
                    act.wait_ge(probs_ready, nth(probs_ready, layer, jobs[jobs.index((kind, h)) - 1]))
                maps = [("A", 0), ("B", 1)] if kind == "diff" else [("AB"[h % 2], 0)]
                for b, m in maps:
                    act.activation(expd[:, m, 0:256], bank[b][:, 0:256], ACT.Exp, bias=nmx[:, m:m + 1],
                                   accum_out=den[:, m:m + 1])
                    last = act.activation(expd[:, m, 256:384], bank[b][:, 256:384], ACT.Exp, bias=nmx[:, 2 + m:3 + m],
                                          accum_out=den[:, 2 + m:3 + m])
                last.then_inc(exped, 1)

            def probs_evac(layer, kind, h):
                act.wait_ge(stage_done, nth(stage_done, layer, ("tr_probs", kind, h)))
                act.activation(probsT[:, :], bank["T"][:, 0:384], ACT.Copy).then_inc(probsT_ready, 1)

            def pv_evac(layer, kind, h):
                if kind == "fox":
                    act.wait_ge(stage_done, nth(stage_done, layer, ("pv", kind, h)))
                    r = (h % 2) * HD
                    lhs_part(layer, ("fox", h), oT[0][r:r + HD, 8 + h // 2, :], bank["O"][r:r + HD, 0:SEQ])

            def diff_evac(layer, t):
                act.wait_ge(stage_done, nth(stage_done, layer, ("tr_diff", t)))
                lhs_part(layer, ("diff", t), oT[0][:, 2:6, t * P:(t + 1) * P],
                         bank["TO"[t]].rearrange("p (h q) -> p h q", h=4), gsub)

            def sigmoid(layer, n):
                for t in range(TT):
                    act.wait_ge(gate_ready, nth(gate_ready, layer, (2 * n + 1, t)))
                    g = wide[:, t, n * D:(n + 1) * D]
                    act.activation(g, g, ACT.Sigmoid).then_inc(gate_open, 1)

            def merged_evac(layer, j):
                for t in range(TT):
                    act.wait_ge(stage_done, nth(stage_done, layer, ("tr_merged", j, t)))
                    lhs_part(layer, ("merged", j, t), hT[0][:, 4 * j:4 * j + 4, t * P:(t + 1) * P],
                             bank[("AB", "TO")[j][t]].rearrange("p (k q) -> p k q", k=4))

            def ff_gate(layer, p):
                item, width = (("ffg", p), NC) if p < NPAIR else ("fflast", 256)
                if p == 0:
                    act.wait_ge(y_ready["ffn"], nth(y_ready["ffn"], layer, "y"))
                for t in range(TT):
                    wait_item(act, layer, item, t)
                    if p >= 2:
                        act.wait_ge(ff_ready, nth(ff_ready, layer, (p - 2, t)))
                    act.activation(ff_tmp(t, p, width), item_bank(layer, ITEM_AT[item], t)[:, 0:width],
                                   ACT.Sigmoid, scale=y_ffn[:, t:t + 1]).then_inc(ff_sig, 1)

            def act_evac(layer, p):
                blocks = 4 if p < NPAIR else 2
                for t in range(TT):
                    act.wait_ge(stage_done, nth(stage_done, layer, ("tr_act", p, t)))
                    lhs_part(layer, ("act", p, t), aT[0][:, 4 * p:4 * p + blocks, t * P:(t + 1) * P],
                             bank[("AB", "TO")[p % 2][t]][:, 0:blocks * P].rearrange("p (k q) -> p k q", k=blocks))

            def nothing(*_):
                pass

            stages = dict(residual=nothing, gain=nothing, maxima=nothing, squares=row_squares, norm_ffn=nothing, norm_evac=norm_evac, qk_norm=qk_norm, pf=pf,
                          fox_forget=fox_forget, qk_evac=qk_evac, cum_evac=nothing, pool_evac_a=pool_evac_a,
                          pool_evac_b=pool_evac_b, ss=ss, ss_evac=ss_evac, sb_logs=sb_logs, svfq=svfq,
                          sb_weights=sb_weights, sb_evac=sb_evac, fox_evac=fox_evac, fkfv=fkfv, dv=dv,
                          softmax=softmax, probs_evac=probs_evac, pv_evac=pv_evac, diff_norm=nothing,
                          diff_evac=diff_evac, gate=nothing, sigmoid=sigmoid, branch=nothing,
                          merged_evac=merged_evac, ff_gate=ff_gate, ff_up=nothing, act_evac=act_evac)
            split_hi(0)
            for b in range(2):
                norm_evac(0, "attn", 0, b)
            for g in range(1, AHEAD):
                split_hi(g)
            for g in range(DEPTH * U):
                layer, u = divmod(g, U)
                for stage, *args in SV_TIMETABLE.get(u, ()):
                    if g == 0 and stage == "norm_evac":
                        continue
                    stages[stage](layer, *args)
                if g + AHEAD < DEPTH * U:
                    split_hi(g + AHEAD)

        @block.vector
        def _(vec):
            steps = [0]

            def count_step():
                steps[0] += 1
                return steps[0]

            def split_lo(g):
                layer, u = divmod(g, U)
                width = sum(w for _, w in ITEMS[UNITS[u][0]][2])
                vec.wait_ge(hi_ready, nth(hi_ready, layer, u))
                vec.tensor_tensor(w_lo[:, g % RING, :, 0:width], raw[:, g % RAW, :, 0:width],
                                                w_hi[:, g % RING, :, 0:width].bitcast(F32), ALU.subtract).then_inc(lo_ready, 1)

            def lhs_rest(layer, event, dst, src, high, scale=None):
                vec.wait_ge(lhs_hi, nth(lhs_hi, layer, event))
                if scale is None:
                    ins = vec.tensor_tensor(dst, src, high.bitcast(F32), ALU.subtract)
                else:
                    ins = vec.scalar_tensor_tensor(out=dst, in0=src, scalar=scale, in1=high.bitcast(F32),
                                                   op0=ALU.mult, op1=ALU.subtract)
                ins.then_inc(lhs_lo, 1)

            m_, h_, y_, a_ = (stat[:, 20 * i:20 * i + 20] for i in range(4))

            def rsqrt(n):
                m, h, y, a = m_[:, 0:n], h_[:, 0:n], y_[:, 0:n], a_[:, 0:n]
                vec.tensor_scalar(h, m, -0.5, None, ALU.mult)
                vec.tensor_scalar(y.bitcast(I32), m.bitcast(I32), -0.5, RSQRT_MAGIC, ALU.mult, ALU.add).then_inc(vec_step, 1)
                vec.wait_ge(vec_step, count_step())
                for _ in range(3):
                    vec.tensor_tensor(a, y, y, ALU.mult).then_inc(vec_step, 1)
                    vec.wait_ge(vec_step, count_step())
                    vec.tensor_tensor(a, a, h, ALU.mult).then_inc(vec_step, 1)
                    vec.wait_ge(vec_step, count_step())
                    vec.scalar_tensor_tensor(out=y, in0=a, scalar=1.5, in1=y, op0=ALU.add, op1=ALU.mult).then_inc(vec_step, 1)
                    vec.wait_ge(vec_step, count_step())

            def mean_square(which, layer, n):
                vec.wait_ge(sumsq[which], nth(sumsq[which], layer, (1, 1)))
                vec.tensor_tensor(m_[:, n:n + TT], ssq[:, :, 0], ssq[:, :, 1], ALU.add).then_inc(vec_step, 1)
                vec.wait_ge(vec_step, count_step())
                vec.tensor_scalar(m_[:, n:n + TT], m_[:, n:n + TT], 1.0 / D, EPS, ALU.mult, ALU.add).then_inc(vec_step, 1)
                vec.wait_ge(vec_step, count_step())

            def residual(layer, which, t, j):
                if layer < 0:
                    return
                wait_item(vec, layer, (which, j), t)
                xs = x_sb[:, t, j * NC:(j + 1) * NC]
                vec.tensor_tensor(xs, item_bank(layer, ITEM_AT[(which, j)], t), xs, ALU.add).then_inc(x_out if which == "out" else x_down, 1)

            def gain(layer, which, t, j):
                if layer == DEPTH:
                    return
                half = slice(j * NC, (j + 1) * NC)
                if which == "ffn":
                    vec.wait_ge(x_out, nth(x_out, layer, (t, j)))
                elif layer:
                    vec.wait_ge(x_down, nth(x_down, layer - 1, (t, j)))
                else:
                    vec.wait_ge(x_loaded[t], 16)
                vec.wait_ge(gain_loaded[which], 16 * (layer + 1))
                vec.tensor_tensor(hn(t)[:, half], x_sb[:, t, half], gain_row[which][:, half], ALU.mult).then_inc(hn_ready[which], 1)

            def norm_ffn(layer):
                mean_square("ffn", layer, 0)
                rsqrt(TT)
                vec.tensor_copy(y_ffn[:, :], y_[:, 0:TT]).then_inc(y_ready["ffn"], 1)
                vec.wait_ge(y_ready["ffn"], nth(y_ready["ffn"], layer, "y"))

            def norm_evac(layer, which, t, b):
                lhs_rest(layer, ("norm", which, t, b), hT[1][:, 4 * b:4 * b + 4, t * P:(t + 1) * P],
                         bank["ABTO"[2 * t + b]].rearrange("p (k q) -> p k q", k=4),
                         hT[0][:, 4 * b:4 * b + 4, t * P:(t + 1) * P])

            def head_norm(layer, which, item, c0, heads):
                width, n = heads * HD, TT * heads
                if which == "dq":
                    mean_square("attn", layer, n)
                    vec.tensor_scalar(eps_heads[:, :], m_[:, n:n + TT], EPS, None, ALU.mult)
                for t in range(TT):
                    vec.wait_ge(squares, nth(squares, layer, (which, t)))
                    last = vec.reduce_sum(m_[:, t * heads:(t + 1) * heads],
                                          scratch(t, SQ, width).rearrange("p (h d) -> p h d", d=HD), AX_X)
                last.then_inc(vec_step, 1)
                vec.wait_ge(vec_step, count_step())
                for t in range(TT):
                    m = m_[:, t * heads:(t + 1) * heads]
                    last = vec.tensor_scalar(m, m, 1.0 / HD, eps_heads[:, t:t + 1], ALU.mult, ALU.add)
                last.then_inc(vec_step, 1)
                vec.wait_ge(vec_step, count_step())
                rsqrt(n + TT if which == "dq" else n)
                for t in range(TT):
                    src = item_bank(layer, ITEM_AT[item], t)[:, c0:c0 + width].rearrange("p (h d) -> p h d", d=HD)
                    vec.tensor_tensor(scratch(t, XN, width).rearrange("p (h d) -> p h d", d=HD), src,
                                      y_[:, t * heads:(t + 1) * heads].unsqueeze(2).broadcast_to([P, heads, HD]),
                                      ALU.mult).then_inc(normed, 1)
                if which == "dq":
                    vec.tensor_copy(y_attn[:, :], y_[:, n:n + TT]).then_inc(y_ready["attn"], 1)
                    vec.wait_ge(y_ready["attn"], nth(y_ready["attn"], layer, "y"))

            def qk_norm(layer, which):
                if which == "dk":
                    for t in range(TT):
                        vec.wait_ge(stage_done, nth(stage_done, layer, ("tr_qk", "dq", t)))
                head_norm(layer, which, which, 0, 8)

            def pf_items(layer):
                for t in range(TT):
                    wait_item(vec, layer, "pf", t)
                    src = item_bank(layer, ITEM_AT["pf"], t)
                    vec.scalar_tensor_tensor(out=fg[:, 4, 4 * t:4 * t + 4], in0=src[:, 256:260], scalar=y_attn[:, t:t + 1], in1=b_f,
                                             op0=ALU.mult, op1=ALU.add).then_inc(vec_step, 1)
                    vec.wait_ge(vec_step, count_step())
                    vec.tensor_scalar(fg[:, 0, 4 * t:4 * t + 4], fg[:, 4, 4 * t:4 * t + 4], -1.0, None, ALU.mult).then_inc(forget_in, 1)

            def lambdas(layer):
                vec.wait_ge(params_loaded, 16 * PARAM_DMAS * (layer + 1))
                tmp = wide[:, 0, 1280:1408].rearrange("p (i d) -> p i d", i=2)
                lv = lamv[:, :, :].rearrange("p (i two) d -> p i two d", two=2)
                vec.tensor_tensor(tmp, lv[:, :, 0, :], lv[:, :, 1, :], ALU.mult).then_inc(vec_step, 1)
                vec.wait_ge(vec_step, count_step())
                vec.reduce_sum(lam_s, tmp, AX_X).then_inc(lam_sum, 1)

            def fox_forget(layer):
                vec.wait_ge(forget_ln, nth(forget_ln, layer, "ln"))
                vec.scalar_tensor_tensor(out=fg[:, 4, :], in0=fg[:, 0, :], scalar=0.0, in1=fg[:, 3, :],
                                                         op0=ALU.max, op1=ALU.add).then_inc(forget_out, 1)
                vec.wait_ge(lam_exp, nth(lam_exp, layer, "exp"))
                vec.tensor_tensor(neglam, lam_e[:, 1:2], lam_e[:, 0:1], ALU.subtract).then_inc(vec_step, 1)
                vec.wait_ge(vec_step, count_step())
                vec.tensor_tensor(neglam, neglam, c("lam")[:, layer:layer + 1], ALU.subtract).then_inc(lam_sum, 1)
                vec.tensor_tensor(gsub, subln, c("one_minus_lam")[:, layer:layer + 1], ALU.mult).then_inc(vec_step, 1)
                vec.wait_ge(vec_step, count_step())

            def cum_evac(layer):
                vec.wait_ge(stage_done, nth(stage_done, layer, ("cum",)))
                neg = bank["T"][:, 0:8].rearrange("p (t h) -> p t h", t=TT)
                vec.tensor_copy(aug["fk"][:, :, :, HD], neg)
                vec.tensor_scalar(aug["fq"][:, :, :, HD + 1], neg, -1.0, None, ALU.mult).then_inc(forget_out, 1)

            def pool_evac_b(layer):
                vec.wait_ge(lhs_hi, nth(lhs_hi, layer, ("pool", 1)))
                for pr in range(2):
                    lhs_rest(layer, ("pool", pr), oT[1][:, pr, :], bank["T"][:, pr * SEQ:(pr + 1) * SEQ], oT[0][:, pr, :],
                             psc[:, pr:pr + 1])

            def sb_logs(layer, pair):
                vec.wait_ge(sb_ln, nth(sb_ln, layer, pair))
                vec.scalar_tensor_tensor(out=sb2[:, :, :], in0=bankAB[:, :, 0:384], scalar=0.0, in1=sb1[:, :, :],
                                         op0=ALU.max, op1=ALU.add).then_inc(vec_step, 1)
                vec.wait_ge(vec_step, count_step())
                vec.tensor_tensor(sb2[:, :, 0:128], sb2[:, :, 0:128],
                                  c("strict").unsqueeze(1).broadcast_to([P, 2, P]), ALU.mult)
                vec.tensor_tensor(sb2[:, :, 256:384], sb2[:, :, 256:384],
                                             c("strict").unsqueeze(1).broadcast_to([P, 2, P]), ALU.mult).then_inc(sb_sp, 1)

            def sb_evac(layer, pair):
                lhs_rest(layer, ("sb", pair), oT[1][:, 6 + pair, :], bank["O"][:, 0:SEQ], oT[0][:, 6 + pair, :])

            def svfq(layer):
                for t in range(TT):
                    vec.wait_ge(stage_done, nth(stage_done, layer, ("tr_qk", "dk", t)))
                head_norm(layer, "fq", "svfq", 256, 4)

            def fkfv(layer):
                for t in range(TT):
                    vec.wait_ge(rotated, nth(rotated, layer, ("fq", t)))
                head_norm(layer, "fk", "fkfv", 0, 4)

            def maxima(layer, kind, h):
                vec.wait_ge(stage_done, nth(stage_done, layer, ("scores", kind, h)))
                mx = row_max[:, :]
                if kind == "diff":
                    vec.reduce_max(mx[:, 0:2], bankAB[:, :, 0:256], AX_X)
                    vec.reduce_max(mx[:, 2:4], bankAB[:, :, 256:384], AX_X).then_inc(vec_step, 1)
                    vec.wait_ge(vec_step, count_step())
                    vec.tensor_scalar(nmx[:, :], mx, -1.0, None, ALU.mult).then_inc(maxed, 1)
                else:
                    b = bank["AB"[h % 2]]
                    vec.reduce_max(mx[:, 0:1], b[:, 0:256], AX_X)
                    vec.reduce_max(mx[:, 2:3], b[:, 256:384], AX_X).then_inc(vec_step, 1)
                    vec.wait_ge(vec_step, count_step())
                    vec.tensor_scalar(nmx[:, 0:3:2], mx[:, 0:3:2], -1.0, None, ALU.mult).then_inc(maxed, 1)

            def softmax(layer, kind, h):
                vec.wait_ge(exped, nth(exped, layer, (kind, h)))
                if (kind, h) != jobs[0]:
                    before = jobs[jobs.index((kind, h)) - 1]
                    vec.wait_ge(stage_done, nth(stage_done, layer, ("tr_probs", *before)))
                r = inverse[:, :]
                if kind == "diff":
                    vec.reciprocal(r, den[:, :]).then_inc(vec_step, 1)
                    vec.wait_ge(vec_step, count_step())
                    vec.tensor_scalar(r[:, 1:4:2], r[:, 1:4:2], neglam, None, ALU.mult).then_inc(vec_step, 1)
                    vec.wait_ge(vec_step, count_step())
                    vec.tensor_scalar(probs[:, 0:256], expd[:, 0, 0:256], r[:, 0:1], None, ALU.mult)
                    vec.tensor_scalar(probs[:, 256:384], expd[:, 0, 256:384], r[:, 2:3], None, ALU.mult).then_inc(vec_step, 1)
                    vec.wait_ge(vec_step, count_step())
                    vec.scalar_tensor_tensor(out=probs[:, 0:256], in0=expd[:, 1, 0:256], scalar=r[:, 1:2],
                                             in1=probs[:, 0:256], op0=ALU.mult, op1=ALU.add)
                    last = vec.scalar_tensor_tensor(out=probs[:, 256:384], in0=expd[:, 1, 256:384], scalar=r[:, 3:4],
                                                    in1=probs[:, 256:384], op0=ALU.mult, op1=ALU.add)
                else:
                    vec.reciprocal(r[:, 0:3:2], den[:, 0:3:2]).then_inc(vec_step, 1)
                    vec.wait_ge(vec_step, count_step())
                    vec.tensor_scalar(probs[:, 0:256], expd[:, 0, 0:256], r[:, 0:1], None, ALU.mult)
                    last = vec.tensor_scalar(probs[:, 256:384], expd[:, 0, 256:384], r[:, 2:3], None, ALU.mult)
                last.then_inc(probs_ready, 1)

            def pv_evac(layer, kind, h):
                if kind == "diff":
                    vec.wait_ge(stage_done, nth(stage_done, layer, ("pv", kind, h)))
                    vec.tensor_copy(o_d[:, :, h, :], bank["O"][:, 0:SEQ].rearrange("p (t d) -> p t d", t=TT)).then_inc(o_d_ready, 1)
                else:
                    r = (h % 2) * HD
                    lhs_rest(layer, ("fox", h), oT[1][r:r + HD, 8 + h // 2, :], bank["O"][r:r + HD, 0:SEQ],
                             oT[0][r:r + HD, 8 + h // 2, :])

            def diff_norm(layer):
                vec.wait_ge(o_sq, nth(o_sq, layer, "squares"))
                for t in range(TT):
                    ins = vec.reduce_sum(m_[:, 4 * t:4 * t + 4], scratch(t, TB).rearrange("p (h d) -> p h d", h=4), AX_X)
                ins.then_inc(vec_step, 1)
                vec.wait_ge(vec_step, count_step())
                vec.tensor_scalar(m_[:, 0:8], m_[:, 0:8], 1.0 / P, EPS, ALU.mult, ALU.add).then_inc(vec_step, 1)
                vec.wait_ge(vec_step, count_step())
                rsqrt(8)
                for t in range(TT):
                    last = vec.tensor_tensor(o_d[:, t, :, :], o_d[:, t, :, :],
                                             y_[:, 4 * t:4 * t + 4].unsqueeze(2).broadcast_to([P, 4, P]), ALU.mult)
                last.then_inc(o_normed, 1)

            def diff_evac(layer, t):
                lhs_rest(layer, ("diff", t), oT[1][:, 2:6, t * P:(t + 1) * P],
                         bank["TO"[t]].rearrange("p (h q) -> p h q", h=4), oT[0][:, 2:6, t * P:(t + 1) * P], gsub)

            def gate(layer, g):
                for t in range(TT):
                    wait_item(vec, layer, ("gate", g), t)
                    vec.wait_ge(bias_loaded[g % 2], 16 * (4 * layer + g // 2 + 1))
                    vec.scalar_tensor_tensor(out=wide[:, t, g * NC:(g + 1) * NC], in0=item_bank(layer, ITEM_AT[("gate", g)], t),
                                             scalar=y_attn[:, t:t + 1], in1=bias[:, g % 2, :], op0=ALU.mult,
                                             op1=ALU.add).then_inc(gate_ready, 1)

            def branch(layer, j, n):
                for t in range(TT):
                    wait_item(vec, layer, ("branch", j, n), t)
                    vec.wait_ge(gate_open, nth(gate_open, layer, (n, t)))
                    g = wide[:, t, n * D + j * NC:n * D + (j + 1) * NC]
                    vec.tensor_tensor(g, item_bank(layer, ITEM_AT[("branch", j, n)], t), g, ALU.mult).then_inc(gated, 1)

            def merged_evac(layer, j):
                for t in range(TT):
                    lhs_rest(layer, ("merged", j, t), hT[1][:, 4 * j:4 * j + 4, t * P:(t + 1) * P],
                             bank[("AB", "TO")[j][t]].rearrange("p (k q) -> p k q", k=4),
                             hT[0][:, 4 * j:4 * j + 4, t * P:(t + 1) * P])

            def ff_gate(layer, p):
                item, width = (("ffg", p), NC) if p < NPAIR else ("fflast", 256)
                for t in range(TT):
                    vec.wait_ge(ff_sig, nth(ff_sig, layer, (p, t)))
                    s = ff_tmp(t, p, width)
                    vec.scalar_tensor_tensor(out=s, in0=item_bank(layer, ITEM_AT[item], t)[:, 0:width], scalar=y_ffn[:, t:t + 1],
                                             in1=s, op0=ALU.mult, op1=ALU.mult).then_inc(ff_gated, 1)

            def ff_up(layer, p):
                item, c0, width = (("ffu", p), 0, NC) if p < NPAIR else ("fflast", 256, 256)
                for t in range(TT):
                    wait_item(vec, layer, item, t)
                    vec.wait_ge(ff_gated, nth(ff_gated, layer, (p, t)))
                    if p >= 2:
                        vec.wait_ge(stage_done, nth(stage_done, layer, ("tr_act", p - 2, t)))
                    vec.scalar_tensor_tensor(out=ff_act(t, p, width), in0=item_bank(layer, ITEM_AT[item], t)[:, c0:c0 + width],
                                             scalar=y_ffn[:, t:t + 1], in1=ff_tmp(t, p, width), op0=ALU.mult,
                                             op1=ALU.mult).then_inc(ff_ready, 1)

            def act_evac(layer, p):
                blocks = 4 if p < NPAIR else 2
                for t in range(TT):
                    dst = slice(4 * p, 4 * p + blocks)
                    lhs_rest(layer, ("act", p, t), aT[1][:, dst, t * P:(t + 1) * P],
                             bank[("AB", "TO")[p % 2][t]][:, 0:blocks * P].rearrange("p (k q) -> p k q", k=blocks),
                             aT[0][:, dst, t * P:(t + 1) * P])

            def pf_all(layer):
                lambdas(layer)
                pf_items(layer)

            def nothing(*_):
                pass

            stages = dict(residual=residual, gain=gain, maxima=maxima, squares=nothing, norm_ffn=norm_ffn, norm_evac=norm_evac, qk_norm=qk_norm, pf=pf_all,
                          fox_forget=fox_forget, qk_evac=nothing, cum_evac=cum_evac, pool_evac_a=nothing,
                          pool_evac_b=pool_evac_b, ss=nothing, ss_evac=nothing, sb_logs=sb_logs, svfq=svfq,
                          sb_weights=nothing, sb_evac=sb_evac, fox_evac=nothing, fkfv=fkfv, dv=nothing,
                          softmax=softmax, probs_evac=nothing, pv_evac=pv_evac, diff_norm=diff_norm,
                          diff_evac=diff_evac, gate=gate, sigmoid=nothing, branch=branch,
                          merged_evac=merged_evac, ff_gate=ff_gate, ff_up=ff_up, act_evac=act_evac)

            for j in range(2):
                gain(0, "attn", 0, j)
            split_lo(0)
            for b in range(2):
                norm_evac(0, "attn", 0, b)
            split_lo(1)
            gain(0, "attn", 1, 0)
            for g in range(2, AHEAD):
                split_lo(g)
            for g in range(DEPTH * U):
                layer, u = divmod(g, U)
                if g == FIRST["ss"]:
                    vec.wait_ge(consts_loaded, 16)
                    for i, name in enumerate(("ident", "causal", "strict_neg")):
                        last = vec.tensor_copy(masks[:, i, :], c(name))
                    last.then_inc(masks_ready, 1)
                for stage, *args in SV_TIMETABLE.get(u, ()):
                    if g == 0 and stage == "norm_evac":
                        continue
                    ahead = stage == "gain" and args[0] == "attn" and u > F0
                    behind = stage == "residual" and args[0] == "down" and u == 0
                    stages[stage](layer + ahead - behind, *args)
                if g + AHEAD < DEPTH * U:
                    split_lo(g + AHEAD)
            residual(DEPTH - 1, "down", 1, 1)

        @block.tensor
        def _(pe):
            identity = c("ident")
            last_read = {b: None for b in "ABTO"}

            def take(banks, *freed):
                for b in banks:
                    if last_read[b] is not None:
                        sig, layer, event = last_read[b]
                        pe.wait_ge(sig, nth(sig, layer, event))
                    last_read[b] = freed

            def tr_norm(layer, which, t, b):
                pe.wait_ge(hn_ready[which], nth(hn_ready[which], layer, (t, b)))
                name = "ABTO"[2 * t + b]
                take(name, lhs_lo, layer, ("norm", which, t, b))
                for k in range(4):
                    ins = pe.transpose(bank[name][:, k * P:(k + 1) * P], hn(t)[:, (4 * b + k) * P:(4 * b + k + 1) * P], identity)
                ins.then_inc(stage_done, 1)

            def tr_qk(layer, which):
                for t in range(TT):
                    pe.wait_ge(rotated, nth(rotated, layer, (which, t)))
                    take("AB"[t], qkT_ready, layer, (which, t))
                    for k in range(4):
                        ins = pe.transpose(bank["AB"[t]][:, k * P:(k + 1) * P], scratch(t, XN)[:, k * P:(k + 1) * P], identity)
                    ins.then_inc(stage_done, 1)

            def tr_fox(layer, which):
                pe.wait_ge(forget_out, nth(forget_out, layer, "aug"))
                for t in range(TT):
                    pe.wait_ge(rotated, nth(rotated, layer, (which, t)))
                    take("AB"[t], qkT_ready, layer, (which, t))
                    for h in range(4):
                        ins = pe.transpose(bank["AB"[t]][0:HD + 2, h * P:(h + 1) * P], aug[which][:, t, h, :], identity)
                    ins.then_inc(stage_done, 1)

            def tr_ss(layer):
                for t in range(TT):
                    pe.wait_ge(ss_staged, nth(ss_staged, layer, t))
                    take("TO"[t], sT_ready, layer, t)
                    for k in range(4):
                        ins = pe.transpose(bank["TO"[t]][:, k * P:(k + 1) * P], scratch(t, SQ)[:, k * P:(k + 1) * P], identity)
                    ins.then_inc(stage_done, 1)

            def cum(layer):
                pe.wait_ge(forget_out, nth(forget_out, layer, "softplus"))
                take("T", forget_out, layer, "aug")
                sp = fg[:, 4, :]
                pe.matmul(bank["T"][:, 0:8], c("upto"), sp, start=True, stop=False, skip_group_check=True)
                ins = pe.matmul(bank["T"][:, 4:8], c("ones"), sp[:, 0:4], start=False, stop=True, skip_group_check=True)
                ins.then_inc(stage_done, 1)

            def pool_a(layer):
                for t in range(TT):
                    pe.wait_ge(u_ready, nth(u_ready, layer, t))
                take("O", pooled, layer, "pooled")
                for g in range(4):
                    r, at = (g % 2) * HD, (g // 2) * SEQ
                    pe.matmul(bank["O"][r:r + HD, at:at + SEQ], pool_u[0][:, g * HD:(g + 1) * HD], c(f"band0_{g}"),
                              start=(g < 2), stop=False, skip_group_check=True)
                    ins = pe.matmul(bank["O"][r:r + HD, at + P:at + SEQ], pool_u[1][:, g * HD:(g + 1) * HD], c(f"band1_{g}"),
                                    start=False, stop=True, skip_group_check=True)
                ins.then_inc(stage_done, 1)

            def pool_b(layer):
                pe.wait_ge(pooled, nth(pooled, layer, "pooled"))
                take("T", lhs_lo, layer, ("pool", 1))
                for pr in range(2):
                    ins = pe.matmul(bank["T"][:, pr * SEQ:(pr + 1) * SEQ], poolw[:, pr, :], pooledT[:, pr * SEQ:(pr + 1) * SEQ],
                                    start=(pr == 0), stop=True, skip_group_check=True)
                ins.then_inc(stage_done, 1)

            def sb_scores(layer, pair):
                for t in range(TT):
                    pe.wait_ge(sT_ready, nth(sT_ready, layer, t))
                take("AB", sb_w, layer, pair)
                for i in range(2):
                    r = slice(i * HD, (i + 1) * HD)
                    b = bank["AB"[i]]
                    pe.matmul(b[:, 0:SEQ], sT[r, 2 + pair, 0:P], sT[r, pair, :], start=True, stop=True, skip_group_check=True)
                    ins = pe.matmul(b[:, SEQ:SEQ + P], sT[r, 2 + pair, P:SEQ], sT[r, pair, P:SEQ], start=False, stop=True,
                                    skip_group_check=True)
                ins.then_inc(stage_done, 1)

            def sb_sums(layer, pair):
                pe.wait_ge(masks_ready, 1)
                pe.wait_ge(sb_sp, nth(sb_sp, layer, pair))
                for i in range(2):
                    b, sp = bank["AB"[i]], sb2[:, i, :]
                    pe.matmul(b[:, 0:SEQ], c("minus_from"), sp[:, 0:SEQ], start=False, stop=False, skip_group_check=True)
                    pe.matmul(b[:, P:SEQ], c("minus_ones"), sp[:, SEQ:SEQ + P], start=False, stop=False, skip_group_check=True)
                    pe.matmul(b[:, SEQ:SEQ + P], c("minus_from"), sp[:, SEQ:SEQ + P], start=False, stop=False, skip_group_check=True)
                    pe.matmul(b[:, 0:P], masks[:, 0, :], masks[:, 2, :], start=False, stop=False, skip_group_check=True)
                    ins = pe.matmul(b[:, SEQ:SEQ + P], masks[:, 0, :], masks[:, 2, :], start=False, stop=True, skip_group_check=True)
                ins.then_inc(stage_done, 1)

            def sb_out(layer, pair):
                pe.wait_ge(sb_w, nth(sb_w, layer, pair))
                pe.wait_ge(v_ready, nth(v_ready, layer, ("sv", 1)))
                take("O", lhs_lo, layer, ("sb", pair))
                for i in range(2):
                    r, h = i * HD, 2 * pair + i
                    pe.matmul(bank["O"][r:r + HD, 0:SEQ], v_s[:, 0, h * HD:(h + 1) * HD], sb1[:, i, 0:SEQ],
                              start=True, stop=False, skip_group_check=True)
                    ins = pe.matmul(bank["O"][r:r + HD, P:SEQ], v_s[:, 1, h * HD:(h + 1) * HD], sb1[:, i, SEQ:SEQ + P],
                                    start=False, stop=True, skip_group_check=True)
                ins.then_inc(stage_done, 1)

            def scores(layer, kind, h):
                pe.wait_ge(masks_ready, 1)
                q, k = ("dq", "dk") if kind == "diff" else ("fq", "fk")
                for w in (q, k):
                    for t in range(TT):
                        pe.wait_ge(qkT_ready, nth(qkT_ready, layer, (w, t)))
                banks = "AB" if kind == "diff" else "AB"[h % 2]
                take(banks, exped, layer, (kind, h))
                for i, name in enumerate(banks):
                    r = slice(i * HD, (i + 1) * HD) if kind == "diff" else slice(0, HD + 2)
                    b = bank[name]
                    pe.matmul(b[:, 0:SEQ], qT[q][r, h, P:SEQ], qT[k][r, h, :], start=True, stop=False, skip_group_check=True)
                    pe.matmul(b[:, SEQ:SEQ + P], qT[q][r, h, 0:P], qT[k][r, h, 0:P], start=False, stop=False, skip_group_check=True)
                    pe.matmul(b[:, P:SEQ], masks[:, 0, :], masks[:, 1, :], start=False, stop=False, skip_group_check=True)
                    ins = pe.matmul(b[:, SEQ:SEQ + P], masks[:, 0, :], masks[:, 1, :], start=False, stop=True, skip_group_check=True)
                ins.then_inc(stage_done, 1)

            def tr_probs(layer, kind, h):
                pe.wait_ge(probs_ready, nth(probs_ready, layer, (kind, h)))
                take("T", probsT_ready, layer, (kind, h))
                for dst, src in ((0, 256), (128, 0), (256, 128)):
                    ins = pe.transpose(bank["T"][:, dst:dst + P], probs[:, src:src + P], identity)
                ins.then_inc(stage_done, 1)

            def pv(layer, kind, h):
                pe.wait_ge(probsT_ready, nth(probsT_ready, layer, (kind, h)))
                if kind == "diff":
                    pe.wait_ge(v_ready, nth(v_ready, layer, ("dv", 1)))
                    take("O", o_d_ready, layer, h)
                    v = [v_d[:, t, h * P:(h + 1) * P] for t in range(TT)]
                    o = bank["O"]
                    pe.matmul(o[:, 0:P], probsT[:, 0:P], v[0], start=True, stop=False, skip_group_check=True)
                    pe.matmul(o[:, P:SEQ], probsT[:, P:SEQ], v[0], start=False, stop=False, skip_group_check=True)
                    ins = pe.matmul(o[:, P:SEQ], probsT[:, SEQ:SEQ + P], v[1], start=False, stop=True, skip_group_check=True)
                else:
                    pe.wait_ge(v_ready, nth(v_ready, layer, ("fv", 1)))
                    take("O", lhs_lo, layer, ("fox", h))
                    r = (h % 2) * HD
                    o = bank["O"][r:r + HD, :]
                    v = [v_f[:, t, h * HD:(h + 1) * HD] for t in range(TT)]
                    pe.matmul(o[:, 0:SEQ], v[0], probsT[:, 0:SEQ], start=True, stop=False, skip_group_check=True)
                    ins = pe.matmul(o[:, P:SEQ], v[1], probsT[:, SEQ:SEQ + P], start=False, stop=True, skip_group_check=True)
                ins.then_inc(stage_done, 1)

            def tr_diff(layer, t):
                pe.wait_ge(o_normed, nth(o_normed, layer, "normed"))
                take("TO"[t], lhs_lo, layer, ("diff", t))
                for h in range(4):
                    ins = pe.transpose(bank["TO"[t]][:, h * P:(h + 1) * P], o_d[:, t, h, :], identity)
                ins.then_inc(stage_done, 1)

            def tr_merged(layer, j):
                for t in range(TT):
                    pe.wait_ge(merged_ready, nth(merged_ready, layer, (j, t)))
                    name = ("AB", "TO")[j][t]
                    take(name, lhs_lo, layer, ("merged", j, t))
                    for k in range(4):
                        ins = pe.transpose(bank[name][:, k * P:(k + 1) * P], merged(t)[:, (4 * j + k) * P:(4 * j + k + 1) * P], identity)
                    ins.then_inc(stage_done, 1)

            def tr_act(layer, p):
                blocks = 4 if p < NPAIR else 2
                for t in range(TT):
                    pe.wait_ge(ff_ready, nth(ff_ready, layer, (p, t)))
                    name = ("AB", "TO")[p % 2][t]
                    take(name, lhs_lo, layer, ("act", p, t))
                    for k in range(blocks):
                        ins = pe.transpose(bank[name][:, k * P:(k + 1) * P], ff_act(t, p, blocks * P)[:, k * P:(k + 1) * P], identity)
                    ins.then_inc(stage_done, 1)

            stages = dict(tr_norm=tr_norm, tr_qk=tr_qk, tr_fox=tr_fox, tr_ss=tr_ss, cum=cum, pool_a=pool_a, pool_b=pool_b,
                          sb_scores=sb_scores, sb_sums=sb_sums, sb_out=sb_out, scores=scores, tr_probs=tr_probs, pv=pv,
                          tr_diff=tr_diff, tr_merged=tr_merged, tr_act=tr_act)

            def lhs_of(name, k, t):
                kind = name if isinstance(name, str) else name[0]
                if kind == "branch":
                    event = (("pool", k) if k < 2 else ("diff", t) if k < 6 else ("sb", k - 6) if k < 8 else ("fox", 2 * (k - 8) + 1))
                    return oT, event
                if kind == "down":
                    return aT, ("act", k // 4, t)
                if kind == "out":
                    return hT, ("merged", k // 4, t)
                which = "ffn" if kind in ("ffg", "ffu", "fflast") else "attn"
                return hT, ("norm", which, t, k // 4)

            reached = {"high": 0, "low": 0}

            def wait_high(layer, event):
                if nth(lhs_hi, layer, event) > reached["high"]:
                    reached["high"] = nth(lhs_hi, layer, event)
                    pe.wait_ge(lhs_hi, nth(lhs_hi, layer, event))

            def wait_low(layer, event):
                if nth(lhs_lo, layer, event) > reached["low"]:
                    reached["low"] = nth(lhs_lo, layer, event)
                    pe.wait_ge(lhs_lo, nth(lhs_lo, layer, event))

            def multiply(g, tiles, high=True, low=True):
                layer, u = divmod(g, U)
                n, k0 = UNITS[u]
                name, _, columns, _ = ITEMS[n]
                ks = item_k(n)
                width = sum(w for _, w in columns)
                if high and k0 == ks[0] and layer * NITEM + n >= 2:
                    before, m = divmod(layer * NITEM + n - 2, NITEM)
                    for t in tiles:
                        sig, event = released_by(ITEMS[m][0], t)
                        pe.wait_ge(sig, nth(sig, before, event))
                for i in range(2):
                    k = k0 + i
                    whi, wlo = w_hi[:, g % RING, i, 0:width], w_lo[:, g % RING, i, 0:width]
                    for t in tiles:
                        operand, event = lhs_of(name, k, t)
                        hi, lo = (part[:, k, t * P:(t + 1) * P] for part in operand)
                        dst = item_bank(layer, n, t)[:, 0:width]
                        if high:
                            if low:
                                wait_low(layer, event)
                            else:
                                wait_high(layer, event)
                            pe.matmul(dst, hi, whi, start=(k == ks[0]), stop=False)
                            pe.matmul(dst, hi, wlo, start=False, stop=False)
                        if low:
                            wait_low(layer, event)
                            ins = pe.matmul(dst, lo, whi, start=False, stop=(k == ks[-1]))
                if low and 1 in tiles:
                    ins.then_inc(unit_done, 1)
                elif low and k == ks[-1]:
                    ins.then_inc(early_done, 1)

            pe.wait_ge(identity_loaded, 16)
            tr_norm(0, *PE_NEXT[1:])
            for layer in range(DEPTH):
                u = 0
                while u < U:
                    if layer == 0 and u == FIRST["pf"]:
                        pe.wait_ge(consts_loaded, 16)
                    for stage, *args in PE_TIMETABLE.get(u, ()):
                        stages[stage](layer, *args)
                    size = GROUPS.get(u, 1)
                    if size == 1:
                        pe.wait_ge(lo_ready, nth(lo_ready, layer, u))
                        multiply(layer * U + u, [0, 1])
                    else:
                        fresh = u in (0, F0)
                        for v in range(u, u + size):
                            pe.wait_ge(lo_ready, nth(lo_ready, layer, v))
                            multiply(layer * U + v, [0], low=not fresh)
                        if fresh:
                            for v in range(u, u + size):
                                multiply(layer * U + v, [0], high=False)
                        for stage, *args in PE_MID.get(u, ()):
                            stages[stage](layer, *args)
                        if u == U - 4 and layer + 1 < DEPTH:
                            tr_norm(layer + 1, *PE_NEXT[1:])
                        for v in range(u, u + size):
                            multiply(layer * U + v, [1])
                    u += size


_INS = ["x", "attn_norm", "ffn_norm", "w_in", "b_gate", "b_forget", "pool_w", "pool_scale", "diff_q_norm",
        "diff_k_norm", "diff_subln", "lam_q1", "lam_k1", "lam_q2", "lam_k2", "fox_q_norm", "fox_k_norm",
        "w_branch", "w_out", "w_ffn_up", "w_ffn_down"]


def kernel(**inputs):
    import concourse.bacc as _bacc
    from concourse.bass_utils import run_bass_kernel_spmd as _run

    nc = _bacc.Bacc("TRN2", target_bir_lowering=False, num_devices=1)
    arrays, args = {}, []
    for name in _INS:
        a = np.ascontiguousarray(inputs[name])
        arrays[f"in_{name}_dram"] = a
        args.append(nc.dram_tensor(f"in_{name}_dram", a.shape, mybir.dt.from_np(a.dtype), kind="ExternalInput").ap())
    consts = np.concatenate(list(constant_blocks().values()), axis=1)
    arrays["consts_dram"] = consts
    args.append(nc.dram_tensor("consts_dram", consts.shape, F32, kind="ExternalInput").ap())
    args.append(nc.dram_tensor("out_dram", (1, SEQ, D), F32, kind="ExternalOutput").ap())
    build(nc, *args)
    r = _run(nc, [arrays], core_ids=[0])
    return r.results[0]["out_dram"]
```

```python
import math
from contextlib import ExitStack

import numpy as np

import concourse.bass as bass
from concourse import mybir

F32 = mybir.dt.float32
F32R = mybir.dt.float32r
BF16 = mybir.dt.bfloat16
I32 = mybir.dt.int32
ALU = mybir.AluOpType
ACT = mybir.ActivationFunctionType
AX_X = mybir.AxisListType.X

P = 128
TT = 2
SEQ = TT * P
DEPTH = 2
D = 1024
KD = D // P
HD = 64
NC = 512
D_FF = 2816
KF = D_FF // P
POOL_WINDOWS = (2, 4, 8, 16)
OFF = dict(u=0, dq=256, dk=768, dv=1280, sq=1792, sv=2304, fk=2816, f=3328, gate=3332)
NEG = -1.0e30
EPS = 1e-6
RSQRT_MAGIC = 1597463007.0

ITEMS = [
    ("dq", "w_in", [(OFF["dq"], 512)], KD),
    ("ss", "w_in", [(OFF["sq"], 512)], KD),
    ("dk", "w_in", [(OFF["dk"], 512)], KD),
    ("svfq", "w_in", [(OFF["sv"], 512)], KD),
    ("fkfv", "w_in", [(OFF["fk"], 512)], KD),
    ("dv", "w_in", [(OFF["dv"], 512)], KD),
    ("pf", "w_in", [(OFF["u"], 256), (OFF["f"], 4)], KD),
]
ITEMS += [(("gate", g), "w_in", [(OFF["gate"] + g * NC, NC)], KD) for g in range(8)]
KB = [range(0, 2), range(2, 6), range(6, 8), range(8, 10)]
ITEMS += [(("branch", j, n), "w_branch", [(j * NC, NC)], KB[n]) for j in range(2) for n in range(4)]
ITEMS += [(("out", j), "w_out", [(j * NC, NC)], KD) for j in range(2)]
NPAIR = 5
for _p in range(NPAIR):
    ITEMS += [(("ffg", _p), "w_up", [(_p * NC, NC)], KD), (("ffu", _p), "w_up", [(D_FF + _p * NC, NC)], KD)]
ITEMS += [("fflast", "w_up", [(NPAIR * NC, 256), (D_FF + NPAIR * NC, 256)], KD)]
ITEMS += [(("down", j), "w_down", [(j * NC, NC)], KF) for j in range(2)]
ITEM_AT = {name: n for n, (name, _, _, _) in enumerate(ITEMS)}
NITEM = len(ITEMS)


def item_k(n):
    k = ITEMS[n][3]
    return list(k) if not isinstance(k, int) else list(range(k))


def plan_units():
    units = []
    n = 0
    while n < NITEM:
        name = ITEMS[n][0]
        if name == ("out", 0):
            units += [(n, 0), (n, 2), (n + 1, 0), (n + 1, 2), (n, 4), (n, 6), (n + 1, 4), (n + 1, 6)]
            n += 2
        elif name == ("down", 0):
            for k in range(0, KF - 4, 2):
                units += [(n, k), (n + 1, k)]
            units += [(n, KF - 4), (n, KF - 2), (n + 1, KF - 4), (n + 1, KF - 2)]
            n += 2
        else:
            units += [(n, k) for k in item_k(n)[::2]]
            n += 1
    return units


UNITS = plan_units()
U = len(UNITS)
FIRST = {}
for _u, (_n, _k) in enumerate(UNITS):
    FIRST.setdefault(ITEMS[_n][0], _u)
LAST = {ITEMS[_n][0]: _u for _u, (_n, _k) in enumerate(UNITS)}
GROUPS = {FIRST["dq"]: 4, LAST[("out", 1)] - 3: 4, FIRST[("ffg", 0)]: 4, U - 4: 4}
RAW = 4
RING = 5
AHEAD = 4
WARM_UP = 50
assert (OFF["gate"] + 8 * NC, U) == (7428, 144)

G0 = FIRST[("gate", 0)]
B0 = FIRST[("branch", 0, 0)]
O0 = FIRST[("out", 0)]
F0 = FIRST[("ffg", 0)]
JOBS = [("diff", h, G0 - 3 + 3 * h) for h in range(4)] + [("fox", h, G0 + 10 + 2 * h) for h in range(4)]


def timetable(*entries):
    table = {}
    for slot, stage, *args in entries:
        table.setdefault(slot, []).append((stage, *args))
    return table


_PE = [(0, "tr_norm", "attn", 0, 1),
       (10, "tr_ss"), (12, "sb_scores", 0), (14, "tr_qk", "dq"), (15, "sb_sums", 0),
       (17, "sb_out", 0), (18, "sb_scores", 1), (21, "sb_sums", 1), (23, "sb_out", 1), (23, "tr_qk", "dk"),
       (31, "cum"), (32, "pool_a"), (34, "pool_b"), (36, "tr_fox", "fq"), (37, "tr_fox", "fk")]
for _kind, _h, _s in JOBS:
    _PE += [(_s, "scores", _kind, _h), (_s + 4, "tr_probs", _kind, _h), (_s + 6, "pv", _kind, _h)]
_PE += [(50, "tr_diff", 0), (51, "tr_diff", 1),
        (B0 + 8, "tr_merged", 0), (O0 + 2, "tr_merged", 1),
        (F0, "tr_norm", "ffn", 0, 1)]
for _p in range(NPAIR):
    _PE += [(FIRST[("ffu", _p)] + 6, "tr_act", _p)]
_PE += [(LAST["fflast"] + 3, "tr_act", NPAIR)]
_PE.sort(key=lambda e: e[0])
PE_TIMETABLE = timetable(*_PE)
BIAS_AT = [G0 + 1 + 4 * g for g in range(8)]
PE_MID = {0: [("tr_norm", "attn", 1, 0), ("tr_norm", "attn", 1, 1)],
          F0 - 4: [("tr_norm", "ffn", 0, 0)],
          F0: [("tr_norm", "ffn", 1, 0), ("tr_norm", "ffn", 1, 1)]}
PE_NEXT = ("tr_norm", "attn", 0, 0)

QK_BANKS = {"dq": "TO", "dk": "AB"}

def stage_parts(stage, *args):
    if stage == "tr_norm":
        which, t, b = args
        return [((stage, which, t, b), "ABTO"[2 * t + b])]
    if stage == "tr_qk":
        return [((stage, args[0], t), QK_BANKS[args[0]][t]) for t in range(TT)]
    if stage == "tr_fox":
        return [((stage, args[0], t), "AB"[t]) for t in range(TT)]
    if stage == "tr_ss":
        return [((stage, t), "TO"[t]) for t in range(TT)]
    if stage in ("cum", "pool_b"):
        return [((stage,), "T")]
    if stage == "pool_a":
        return [((stage,), "O")]
    if stage in ("sb_scores", "sb_sums"):
        return [((stage, args[0]), "AB")]
    if stage == "sb_out":
        return [((stage, args[0]), "O")]
    if stage == "scores":
        kind, h = args
        return [((stage, kind, h), "AB" if kind == "diff" else "AB"[h % 2])]
    if stage == "tr_probs":
        return [((stage, *args), "T")]
    if stage == "pv":
        return [((stage, *args), "O")]
    if stage == "tr_diff":
        return [((stage, args[0]), "TO"[args[0]])]
    if stage == "tr_merged":
        return [((stage, args[0], t), ("AB", "TO")[args[0]][t]) for t in range(TT)]
    if stage == "tr_act":
        return [((stage, args[0], t), ("AB", "TO")[args[0] % 2][t]) for t in range(TT)]
    raise ValueError(stage)


STAGE_EVENTS = [e for e, _ in stage_parts(*PE_NEXT)]
for _u in range(U):
    for _s in PE_TIMETABLE.get(_u, []) + PE_MID.get(_u, []):
        STAGE_EVENTS += [e for e, _ in stage_parts(*_s)]


EARLY = [name for g, size in GROUPS.items() for name, last in LAST.items() if g <= last < g + size]


_SV = [(0, "norm_evac", "attn", 0, 0), (0, "norm_evac", "attn", 0, 1), (0, "squares", "attn", 0), (0, "residual", "down", 1, 1), (0, "gain", "attn", 1, 1),
       (1, "norm_evac", "attn", 1, 0), (1, "norm_evac", "attn", 1, 1), (1, "squares", "attn", 1),
       (4, "qk_norm", "dq"), (8, "ss"), (9, "lambda_sums"), (10, "ss_evac"), (10, "lambdas"),
       (12, "sb_logs", 0), (12, "sb_split", 0), (12, "qk_norm", "dk"), (14, "qk_evac", "dq"), (15, "sb_weights", 0),
       (16, "svfq"), (17, "sb_evac", 0), (18, "sb_logs", 1), (18, "sb_split", 1), (20, "fkfv"), (21, "sb_weights", 1),
       (23, "sb_evac", 1), (23, "qk_evac", "dk"), (24, "dv"),
       (28, "pf"), (29, "fox_forget"), (31, "cum_evac"), (32, "pool_evac_a"), (34, "pool_evac_b"),
       (36, "fox_evac", "fq"), (37, "fox_evac", "fk")]
for _kind, _h, _s in JOBS:
    _SV += [(_s, "maxima", _kind, _h), (_s + 1, "softmax", _kind, _h), (_s + 4, "probs_evac", _kind, _h),
            (_s + 6, "pv_evac", _kind, _h)]
_SV += [(46, "diff_norm"), (50, "diff_evac", 0), (51, "diff_evac", 1)]
for _g in range(8):
    _SV += [(FIRST[("gate", _g)] + 4, "gate", _g)]
_SV += [((46, 48, 53)[n] + t, "sigmoid", n, t) for n in range(3) for t in range(TT)]
_SV += [(B0 + 1, "sigmoid", 3, 0), (B0 + 1, "sigmoid", 3, 1)]
for _j in range(2):
    for _n in range(4):
        _SV += [(LAST[("branch", _j, _n)] + 1, "branch", _j, _n)]
_SV += [(B0 + 8, "merged_evac", 0), (O0 + 2, "merged_evac", 1),
        (F0 - 3, "residual", "out", 0, 0), (F0 - 3, "gain", "ffn", 0, 0),
        (F0 - 3, "residual", "out", 0, 1), (F0 - 3, "gain", "ffn", 0, 1),
        (F0 - 1, "residual", "out", 1, 0), (F0 - 1, "gain", "ffn", 1, 0),
        (F0, "norm_evac", "ffn", 0, 0), (F0, "norm_evac", "ffn", 0, 1), (F0, "squares", "ffn", 0), (F0, "residual", "out", 1, 1), (F0, "gain", "ffn", 1, 1),
        (F0 + 1, "norm_evac", "ffn", 1, 0), (F0 + 1, "norm_evac", "ffn", 1, 1), (F0 + 1, "squares", "ffn", 1), (F0 + 2, "norm_ffn")]
for _p in range(NPAIR):
    _SV += [(FIRST[("ffu", _p)], "ff_gate", _p), (FIRST[("ffu", _p)] + 4, "ff_up", _p),
            (FIRST[("ffu", _p)] + 6, "act_evac", _p)]
_SV += [(LAST["fflast"] + 1, "ff_gate", NPAIR), (LAST["fflast"] + 1, "ff_up", NPAIR),
        (LAST["fflast"] + 3, "act_evac", NPAIR),
        (U - 3, "residual", "down", 0, 0), (U - 3, "gain", "attn", 0, 0),
        (U - 3, "residual", "down", 0, 1), (U - 3, "gain", "attn", 0, 1),
        (U - 1, "residual", "down", 1, 0), (U - 1, "gain", "attn", 1, 0)]
_SV.sort(key=lambda e: e[0])
SV_TIMETABLE = timetable(*_SV)
_ORDER = [tuple(e[1:]) for e in _SV]


def evac_events():
    out = []
    for s in _ORDER:
        if s[0] == "norm_evac":
            out += [("norm", *s[1:])]
        elif s[0] == "pool_evac_b":
            out += [("pool", 0), ("pool", 1)]
        elif s[0] == "sb_evac":
            out += [("sb", s[1])]
        elif s[0] == "pv_evac" and s[1] == "fox":
            out += [("fox", s[2])]
        elif s[0] == "diff_evac":
            out += [("diff", s[1])]
        elif s[0] == "merged_evac":
            out += [("merged", s[1], t) for t in range(TT)]
        elif s[0] == "act_evac":
            out += [("act", s[1], t) for t in range(TT)]
    return out


def constant_blocks():
    q = np.arange(P)
    key, col = q[:, None], q[None, :]
    blocks = {}
    blocks["ident"] = np.eye(P)
    blocks["causal"] = np.where(col > key, NEG, 0.0)
    blocks["strict_neg"] = np.where(key >= col, NEG, 0.0)
    blocks["strict"] = (key < col) * 1.0
    blocks["minus_upto"] = (key <= col) * -1.0
    blocks["minus_from"] = (key >= col) * -1.0
    blocks["minus_ones"] = -np.ones((P, P))
    half = HD // 2
    inv = np.float32(10000.0) ** (-np.arange(half, dtype=np.float32) / np.float32(half))
    ang = np.arange(SEQ, dtype=np.float32)[:, None] * inv[None, :]
    cos, sin = np.cos(ang), np.sin(ang)
    cc = np.concatenate([cos, cos], 1).reshape(TT, P, HD)
    ss = np.concatenate([-sin, sin], 1).reshape(TT, P, HD)
    blocks["cos"] = cc.transpose(1, 0, 2).reshape(P, -1)
    blocks["sin"] = ss.transpose(1, 0, 2).reshape(P, -1)
    lam = [0.8 - 0.6 * math.exp(-0.3 * layer) for layer in range(DEPTH)]
    blocks["lam"] = np.tile(np.array(lam), (P, 1))
    blocks["one_minus_lam"] = np.tile(1.0 - np.array(lam), (P, 1))
    src, dst = np.arange(SEQ)[:, None], np.arange(SEQ)[None, :]
    for g, w in enumerate(POOL_WINDOWS):
        band = ((src <= dst) & (src > dst - w)) / np.minimum(dst + 1, w) - (src == dst)
        blocks[f"band0_{g}"] = band[0:P, :]
        blocks[f"band1_{g}"] = band[P:, P:]
    return {n: np.ascontiguousarray(b, dtype=np.float32) for n, b in blocks.items()}


def build(nc, x, attn_norm, ffn_norm, w_in, b_gate, b_forget, pool_w, pool_scale, diff_q_norm,
          diff_k_norm, diff_subln, lam_q1, lam_k1, lam_q2, lam_k2, fox_q_norm, fox_k_norm,
          w_branch, w_out, w_ffn_up, w_ffn_down, consts, out):
    cblocks = constant_blocks()
    ccol, ncol = {}, 0
    for name, block in cblocks.items():
        ccol[name] = (ncol, block.shape[1])
        ncol += block.shape[1]
    first_band = ccol["band0_0"][0]
    weights = {"w_in": w_in, "w_branch": w_branch, "w_out": w_out, "w_up": w_ffn_up, "w_down": w_ffn_down}

    with ExitStack() as ctx:
        def sb(name, shape, dt=F32, stack=ctx):
            return stack.enter_context(nc.sbuf_tensor(name, shape, dt))

        event_order = {}

        def signal(name, events):
            events = list(events)
            semaphore = ctx.enter_context(nc.semaphore(name))
            event_order[id(semaphore)] = {e: i + 1 for i, e in enumerate(events)}
            assert len(event_order[id(semaphore)]) == len(events)
            return semaphore

        def nth(semaphore, layer, event):
            order_in_layer = event_order[id(semaphore)]
            return layer * len(order_in_layer) + order_in_layer[event]

        def sem(name):
            return ctx.enter_context(nc.semaphore(name))

        raw = sb("raw", [P, RAW, 2, NC])
        w_hi = sb("w_hi", [P, RING, 2, NC], F32R)
        w_lo = sb("w_lo", [P, RING, 2, NC], F32R)
        x_sb = sb("x_sb", [P, TT, D])
        hT = [sb("hT_hi", [P, KD, SEQ], F32R), sb("hT_lo", [P, KD, SEQ], F32R)]
        wide = sb("wide", [P, TT, 4 * D])
        con = sb("con", [P, ncol])
        masks = sb("masks", [P, 3, P], BF16)
        sums = sb("sums", [P, 2, P], F32R)
        bias = sb("bias", [P, 2, NC])
        gains = sb("gains", [P, 4, HD])
        ropeA = sb("ropeA", [P, 2, TT, HD])
        ropeB = sb("ropeB", [P, 2, TT, HD])
        lamv = sb("lamv", [P, 4, HD])
        poolw = sb("poolw", [P, 2, P])
        small = sb("small", [P, 16])
        b_f, psc, subln = small[:, 0:4], small[:, 4:6], small[:, 6:7]
        gsub, neglam, lam_e, lam_s = small[:, 7:8], small[:, 8:9], small[:, 9:11], small[:, 11:13]
        warm = sb("warm", [P, P], BF16)
        stat = sb("stat", [P, 80])
        eps_heads = sb("eps_heads", [P, TT])
        row_max = sb("row_max", [P, 4])
        inverse = sb("inverse", [P, 4])
        y_norm = {"attn": sb("y_attn", [P, TT]), "ffn": sb("y_ffn", [P, TT])}
        ssq = sb("ssq", [P, TT, 2])
        nmx = sb("nmx", [P, 4])
        den = sb("den", [P, 4])
        fg = sb("fg", [P, 5, 8])
        mixing = ExitStack()
        oT = [sb("oT_hi", [P, 10, SEQ], F32R, mixing), sb("oT_lo", [P, 10, SEQ], F32R, mixing)]
        queries = [sb(f"queries_{part}", [P, 4, SEQ], F32R, mixing) for part in ("hi", "lo")]
        keys = [sb(f"keys_{part}", [P, 4, SEQ], F32R, mixing) for part in ("hi", "lo")]
        qT = {"dq": queries, "dk": keys, "fq": queries, "fk": keys}
        sT = keys
        sticks = ExitStack()
        softplus = [sb(f"softplus_{part}", [P, 2, 384], F32R, sticks) for part in ("hi", "lo")]
        sticks.close()
        v_d = sb("v_d", [P, TT, 512], F32, mixing)
        o_d = sb("o_d", [P, TT, 4, P], F32, mixing)
        v_s = sb("v_s", [P, TT, 256], F32, mixing)
        v_f = sb("v_f", [P, TT, 256], F32, mixing)
        aug = {"fq": sb("q_aug", [P, TT, 4, HD + 2], F32, mixing), "fk": sb("k_aug", [P, TT, 4, HD + 2], F32, mixing)}
        sb1 = sb("sb1", [P, 2, 384], F32, mixing)
        sb2 = sb("sb2", [P, 2, 384], F32, mixing)
        expd = sb2
        probs = sb("probs", [P, 384], F32, mixing)
        probsT = sb("probsT", [P, 384], F32, mixing)
        mixing.close()
        ffn_area = ExitStack()
        aT = [sb("aT_hi", [P, KF, SEQ], F32R, ffn_area), sb("aT_lo", [P, KF, SEQ], F32R, ffn_area)]
        ffn_area.close()

        def scratch(t, n, width=512):
            return wide[:, t, 2048 + n * 512:2048 + n * 512 + width]
        XN, TA, TB, SQ = range(4)

        def xn(which, t):
            at, width = {"dq": (2048, 512), "dk": (0, 512), "fq": (512, 256), "fk": (768, 256)}[which]
            return wide[:, t, at:at + width]
        pool_u = [wide[:, t, 1024:1280] for t in range(TT)]
        pooledT = wide[:, 0, 1536:2048]

        def hn(t):
            return wide[:, t, 0:D]
        gain_row = {"ffn": wide[:, 0, D:2 * D], "attn": wide[:, 1, D:2 * D]}

        def merged(t):
            return wide[:, t, 0:D]

        def ff_tmp(t, p, width):
            return wide[:, t, 2048 + 1024 * (p % 2):2048 + 1024 * (p % 2) + width]

        def ff_act(t, p, width):
            return wide[:, t, 2560 + 1024 * (p % 2):2560 + 1024 * (p % 2) + width]

        def c(name):
            a, w = ccol[name]
            return con[:, a:a + w]

        bulk = ctx.enter_context(nc.psum_tensor("bulk", [P, 2, TT, NC], F32))
        bankAB = ctx.enter_context(nc.psum_tensor("bankAB", [P, 2, NC], F32))
        bankT = ctx.enter_context(nc.psum_tensor("bankT", [P, NC], F32))
        bankO = ctx.enter_context(nc.psum_tensor("bankO", [P, NC], F32))
        bank = {"A": bankAB[:, 0, :], "B": bankAB[:, 1, :], "T": bankT[:, :], "O": bankO[:, :]}

        y_attn, y_ffn = y_norm["attn"], y_norm["ffn"]

        def item_bank(layer, n, t):
            return bulk[:, (layer * NITEM + n) % 2, t, :]

        raw_loaded = [sem(f"raw_loaded{s}") for s in range(RAW)]
        hi_ready = signal("hi_ready", range(U))
        lo_ready = signal("lo_ready", range(U))
        unit_done = signal("unit_done", range(U))
        early_done = signal("early_done", EARLY)
        stage_done = signal("stage_done", STAGE_EVENTS)
        evacs = evac_events()
        lhs_hi = signal("lhs_hi", evacs)
        lhs_lo = signal("lhs_lo", evacs)
        warm_ready, bands_loaded = sem("warm_ready"), sem("bands_loaded")
        identity_loaded, consts_loaded, params_loaded = sem("identity_loaded"), sem("consts_loaded"), sem("params_loaded")
        x_loaded = [sem("x_loaded0"), sem("x_loaded1")]
        gain_loaded = {"attn": sem("attn_gain_loaded"), "ffn": sem("ffn_gain_loaded")}
        bias_loaded = [sem("bias_loaded0"), sem("bias_loaded1")]
        stored = sem("stored")
        masks_ready, fills_ready = sem("masks_ready"), sem("fills_ready")
        act_step, vec_step, pool_step = sem("act_step"), sem("vec_step"), sem("pool_step")
        squares = signal("squares", [(w, t) for w in ("dq", "dk", "fq", "fk") for t in range(TT)])
        normed = signal("normed", [(w, t) for w in ("dq", "dk", "fq", "fk") for t in range(TT)])
        rotated = signal("rotated", [(w, t) for w in ("dq", "dk", "fq", "fk") for t in range(TT)])
        tables_ready = signal("tables_ready", ["rope"])
        u_ready = signal("u_ready", range(TT))
        forget_in = signal("forget_in", range(TT))
        forget_ln = signal("forget_ln", ["ln"])
        forget_out = signal("forget_out", ["softplus", "aug"])
        pooled = signal("pooled", ["pooled"])
        qkT_ready = signal("qkT_ready", [(w, t) for w in ("dq", "dk", "fq", "fk") for t in range(TT)])
        qkT_hi = signal("qkT_hi", [(w, t) for w in ("dq", "dk", "fq", "fk") for t in range(TT)])
        sT_hi = signal("sT_hi", range(TT))
        ss_staged = signal("ss_staged", range(TT))
        sT_ready = signal("sT_ready", range(TT))
        sb_ln = signal("sb_ln", range(2))
        sb_sp = signal("sb_sp", range(2))
        sb_hi = signal("sb_hi", range(2))
        sb_lo = signal("sb_lo", range(2))
        sb_w = signal("sb_w", range(2))
        v_ready = signal("v_ready", [(v, t) for v in ("sv", "fv", "dv") for t in range(TT)])
        jobs = [(k, h) for k, h, _ in JOBS]
        maxed = signal("maxed", jobs)
        exped = signal("exped", jobs)
        probs_ready = signal("probs_ready", jobs)
        probsT_ready = signal("probsT_ready", jobs)
        o_d_ready = signal("o_d_ready", range(4))
        o_sq = signal("o_sq", ["squares"])
        o_normed = signal("o_normed", ["normed"])
        lam_exp = signal("lam_exp", ["exp"])
        lam_sum = signal("lam_sum", ["sum", "lam"])
        gate_ready = signal("gate_ready", [(g, t) for g in range(8) for t in range(TT)])
        gate_open = signal("gate_open", [(n, t) for n in range(4) for t in range(TT)])
        gated = signal("gated", [(j, n, t) for j in range(2) for n in range(4) for t in range(TT)])
        summed = signal("summed", [(j, n) for j in range(2) for n in (1, 2)])
        merged_ready = signal("merged_ready", [(j, t) for j in range(2) for t in range(TT)])
        x_out = signal("x_out", [(t, j) for t in range(TT) for j in range(2)])
        x_down = signal("x_down", [(t, j) for t in range(TT) for j in range(2)])
        sumsq = {w: signal(f"sumsq_{w}", [(t, j) for t in range(TT) for j in range(2)]) for w in ("attn", "ffn")}
        hn_ready = {w: signal(f"hn_ready_{w}", [(t, j) for t in range(TT) for j in range(2)]) for w in ("attn", "ffn")}
        y_ready = {w: signal(f"y_ready_{w}", ["y"]) for w in ("attn", "ffn")}
        ff_sig = signal("ff_sig", [(p, t) for p in range(NPAIR + 1) for t in range(TT)])
        ff_gated = signal("ff_gated", [(p, t) for p in range(NPAIR + 1) for t in range(TT)])
        ff_ready = signal("ff_ready", [(p, t) for p in range(NPAIR + 1) for t in range(TT)])

        def wait_item(engine, layer, name, t):
            if t == 0 and name in EARLY:
                engine.wait_ge(early_done, nth(early_done, layer, name))
            else:
                engine.wait_ge(unit_done, nth(unit_done, layer, LAST[name]))

        def released_by(name, t):
            return {
                "dq": (normed, ("dq", t)), "pf": (u_ready, t), "dk": (normed, ("dk", t)), "ss": (ss_staged, t),
                "svfq": (normed, ("fq", t)), "fkfv": (normed, ("fk", t)), "dv": (v_ready, ("dv", t)),
                "gate": (gate_ready, (name[1], t)), "branch": (gated, (*name[1:], t)),
                "out": (x_out, (t, name[1])), "down": (x_down, (t, name[1])),
                "ffg": (ff_gated, (name[1], t)), "ffu": (ff_ready, (name[1], t)), "fflast": (ff_ready, (NPAIR, t)),
            }[name if isinstance(name, str) else name[0]]

        PARAM_DMAS = 16

        block = ctx.enter_context(nc.Block())

        @block.sync
        def _(sp):
            filled = [0] * RAW

            def load_unit(g):
                layer, u = divmod(g, U)
                n, k = UNITS[u]
                name, matrix, columns, _ = ITEMS[n]
                if g >= RAW:
                    sp.wait_ge(lo_ready, nth(lo_ready, *divmod(g - RAW, U)))
                rows = weights[matrix][layer, k * P:(k + 2) * P, :].rearrange("(k p) n -> p k n", p=P)
                at = 0
                for c0, w in columns:
                    sp.dma_start(raw[:, g % RAW, :, at:at + w], rows[:, :, c0:c0 + w]).then_inc(raw_loaded[g % RAW], 16)
                    at += w
                    filled[g % RAW] += 16

            def load_param(layer, n):
                if layer and n == 0:
                    sp.wait_ge(gated, nth(gated, layer - 1, (1, 3, 1)))
                if n < 4:
                    g = (diff_q_norm, diff_k_norm, fox_q_norm, fox_k_norm)[n]
                    dst, src = gains[:, n, :], g[layer].partition_broadcast(P)
                elif n < 8:
                    g = (lam_q1, lam_k1, lam_q2, lam_k2)[n - 4]
                    dst, src = lamv[:, n - 4, :], g[layer].partition_broadcast(P)
                elif n < 12:
                    g, r = n - 8, (n % 2) * HD
                    dst, src = poolw[r:r + HD, g // 2, r:r + HD], pool_w[layer, g]
                elif n < 14:
                    i = n - 12
                    dst, src = psc[:, i:i + 1], pool_scale[layer, i * P:(i + 1) * P].rearrange("(p c) -> p c", c=1)
                elif n == 14:
                    dst, src = b_f, b_forget[layer].partition_broadcast(P)
                else:
                    dst, src = subln, diff_subln[layer].rearrange("(p c) -> p c", c=1)
                sp.dma_start(dst, src).then_inc(params_loaded, 16)

            sp.dma_start(x_sb[:, 0, :], x[0, 0:P, :]).then_inc(x_loaded[0], 16)
            sp.dma_start(gain_row["attn"], attn_norm[0].partition_broadcast(P)).then_inc(gain_loaded["attn"], 16)
            sp.dma_start(con[:, 0:P], consts[:, 0:P]).then_inc(identity_loaded, 16)
            for g in range(RAW):
                if g == 2:
                    sp.dma_start(x_sb[:, 1, :], x[0, P:SEQ, :]).then_inc(x_loaded[1], 16)
                load_unit(g)
            sp.wait_ge(fills_ready, 1)
            for layer in range(DEPTH):
                for u in range(U):
                    if u in BIAS_AT:
                        g = BIAS_AT.index(u)
                        if g >= 2:
                            sp.wait_ge(gate_ready, nth(gate_ready, layer, (g - 2, 1)))
                        elif layer:
                            sp.wait_ge(gate_ready, nth(gate_ready, layer - 1, (6 + g, 1)))
                        sp.dma_start(bias[:, g % 2, :], b_gate[layer, g // 2, (g % 2) * NC:(g % 2 + 1) * NC]
                                     .partition_broadcast(P)).then_inc(bias_loaded[g % 2], 16)
                    if u == O0 + 5:
                        sp.wait_ge(summed, nth(summed, layer, (1, 1)))
                        sp.dma_start(gain_row["ffn"], ffn_norm[layer].partition_broadcast(P)) \
                            .then_inc(gain_loaded["ffn"], 16)
                        if layer + 1 < DEPTH:
                            sp.dma_start(gain_row["attn"], attn_norm[layer + 1].partition_broadcast(P)) \
                                .then_inc(gain_loaded["attn"], 16)
                    if layer + 1 < DEPTH and F0 + 8 <= u < F0 + 8 + PARAM_DMAS:
                        load_param(layer + 1, u - F0 - 8)
                    if layer * U + u + RAW < DEPTH * U:
                        load_unit(layer * U + u + RAW)
                    if layer == 0:
                        if u == 1:
                            sp.dma_start(con[:, P:first_band], consts[:, P:first_band]).then_inc(consts_loaded, 16)
                        if u == 3:
                            sp.dma_start(con[:, first_band:ncol], consts[:, first_band:ncol]).then_inc(bands_loaded, 16)
                        if 2 <= u < 6:
                            for n in range(4 * (u - 2), 4 * (u - 1)):
                                load_param(0, n)
            for t in range(TT):
                for j in range(2):
                    half = slice(j * NC, (j + 1) * NC)
                    sp.wait_ge(x_down, nth(x_down, DEPTH - 1, (t, j)))
                    sp.dma_start(out[0, t * P:(t + 1) * P, half], x_sb[:, t, half]).then_inc(stored, 16)
            sp.wait_ge(stored, 16 * 2 * TT)

        @block.gpsimd
        def _(pool):
            steps = [0]

            def count_step():
                steps[0] += 1
                return steps[0]

            pool.memset(poolw[:, :, :], 0.0).then_inc(pool_step, 1)
            pool.wait_ge(pool_step, count_step())
            pool.memset(aug["fq"][:, :, :, HD:HD + 1], 1.0).then_inc(pool_step, 1)
            pool.wait_ge(pool_step, count_step())
            pool.memset(aug["fk"][:, :, :, HD + 1:HD + 2], 1.0).then_inc(fills_ready, 1)
            pool.wait_ge(consts_loaded, 16)
            cos = c("cos").rearrange("p (t d) -> p t d", t=TT)
            sin = c("sin").rearrange("p (t d) -> p t d", t=TT)
            half = HD // 2
            for layer in range(DEPTH):
                pool.wait_ge(params_loaded, 16 * PARAM_DMAS * (layer + 1))
                for i in range(2):
                    g = gains[:, i:i + 1, :].broadcast_to([P, TT, HD])
                    pool.tensor_tensor(ropeA[:, i, :, :], cos, g, ALU.mult)
                    pool.tensor_tensor(ropeB[:, i, :, 0:half], sin[:, :, 0:half], g[:, :, half:HD], ALU.mult)
                    last = pool.tensor_tensor(ropeB[:, i, :, half:HD], sin[:, :, half:HD], g[:, :, 0:half], ALU.mult)
                last = pool.tensor_scalar(gains[:, 2, :], gains[:, 2, :], HD ** -0.5, None, ALU.mult)
                last.then_inc(tables_ready, 1)
                pool.wait_ge(tables_ready, nth(tables_ready, layer, "rope"))

                def rotate(which, t):
                    i = ("dq", "dk").index(which)
                    pool.wait_ge(normed, nth(normed, layer, (which, t)))
                    x = xn(which, t).rearrange("p (h d) -> p h d", d=HD)
                    ta = scratch(t, TA).rearrange("p (h d) -> p h d", d=HD)
                    tb = scratch(t, TB).rearrange("p (h d) -> p h d", d=HD)
                    pool.tensor_tensor(ta, x, ropeA[:, i, t:t + 1, :].broadcast_to([P, 8, HD]), ALU.mult)
                    pool.tensor_tensor(tb[:, :, 0:half], x[:, :, half:HD],
                                       ropeB[:, i, t:t + 1, 0:half].broadcast_to([P, 8, half]), ALU.mult)
                    pool.tensor_tensor(tb[:, :, half:HD], x[:, :, 0:half],
                                       ropeB[:, i, t:t + 1, half:HD].broadcast_to([P, 8, half]), ALU.mult) \
                                           .then_inc(pool_step, 1)
                    pool.wait_ge(pool_step, count_step())
                    pool.tensor_tensor(x, ta, tb, ALU.add).then_inc(rotated, 1)

                def fox_gain(which, t):
                    i = 2 + ("fq", "fk").index(which)
                    pool.wait_ge(normed, nth(normed, layer, (which, t)))
                    pool.tensor_tensor(
                        aug[which][:, t, :, 0:HD], xn(which, t).rearrange("p (h d) -> p h d", d=HD),
                        gains[:, i:i + 1, :].broadcast_to([P, 4, HD]), ALU.mult).then_inc(rotated, 1)

                for which in ("dq", "dk"):
                    for t in range(TT):
                        rotate(which, t)
                for which in ("fq", "fk"):
                    for t in range(TT):
                        fox_gain(which, t)
                pool.wait_ge(o_d_ready, nth(o_d_ready, layer, 3))
                for t in range(TT):
                    last = pool.tensor_tensor(scratch(t, TB).rearrange("p (h d) -> p h d", h=4),
                                              o_d[:, t, :, :], o_d[:, t, :, :], ALU.mult)
                last.then_inc(o_sq, 1)
                for j in range(2):
                    for n in range(1, 4):
                        for t in range(TT):
                            pool.wait_ge(gated, nth(gated, layer, (j, n, t)))
                            m = merged(t)[:, j * NC:(j + 1) * NC]
                            ins = pool.tensor_tensor(m, m, wide[:, t, n * D + j * NC:n * D + (j + 1) * NC], ALU.add)
                            if n == 3:
                                ins.then_inc(merged_ready, 1)
                            elif t == 1:
                                ins.then_inc(summed, 1)
                                pool.wait_ge(summed, nth(summed, layer, (j, n)))

        @block.scalar
        def _(act):
            steps = [0]

            def count_step():
                steps[0] += 1
                return steps[0]

            loaded = [0] * RAW

            def split_hi(g):
                layer, u = divmod(g, U)
                width = sum(w for _, w in ITEMS[UNITS[u][0]][2])
                loaded[g % RAW] += 16 * len(ITEMS[UNITS[u][0]][2])
                act.wait_ge(raw_loaded[g % RAW], loaded[g % RAW])
                if g >= RING:
                    act.wait_ge(unit_done, nth(unit_done, *divmod(g - RING, U)))
                act.activation(w_hi[:, g % RING, :, 0:width], raw[:, g % RAW, :, 0:width], ACT.Copy).then_inc(hi_ready, 1)

            def lhs_part(layer, event, dst, src, scale=None):
                ins = act.activation(dst, src, ACT.Copy) if scale is None else act.activation(dst, src, ACT.Copy, scale=scale)
                ins.then_inc(lhs_hi, 1)

            def row_squares(layer, which, t):
                for j in range(2):
                    if which == "ffn":
                        act.wait_ge(x_out, nth(x_out, layer, (t, j)))
                    elif layer:
                        act.wait_ge(x_down, nth(x_down, layer - 1, (t, j)))
                    elif j == 0:
                        act.wait_ge(x_loaded[t], 16)
                    act.activation(scratch(t, 2 + j), x_sb[:, t, j * NC:(j + 1) * NC],
                                   ACT.Square, accum_out=ssq[:, t, j:j + 1]).then_inc(sumsq[which], 1)

            def norm_evac(layer, which, t, b):
                act.wait_ge(stage_done, nth(stage_done, layer, ("tr_norm", which, t, b)))
                lhs_part(layer, ("norm", which, t, b), hT[0][:, 4 * b:4 * b + 4, t * P:(t + 1) * P],
                         bank["ABTO"[2 * t + b]].rearrange("p (k q) -> p k q", k=4))

            def head_squares(layer, which, item, c0, width, copy_to=None):
                for t in range(TT):
                    wait_item(act, layer, item, t)
                    src = item_bank(layer, ITEM_AT[item], t)
                    if copy_to is not None:
                        act.activation(copy_to[:, t, :], src[:, 256 - c0:512 - c0], ACT.Copy, scale=y_attn[:, t:t + 1]) \
                            .then_inc(v_ready, 1)
                    act.activation(scratch(t, SQ, width), src[:, c0:c0 + width], ACT.Square).then_inc(squares, 1)

            def qk_norm(layer, which):
                if which == "dk":
                    act.wait_ge(stage_done, nth(stage_done, layer, ("tr_ss", 1)))
                else:
                    act.wait_ge(sumsq["attn"], nth(sumsq["attn"], layer, (1, 1)))
                head_squares(layer, which, which, 0, 512)

            def fox_forget(layer):
                act.wait_ge(forget_in, nth(forget_in, layer, 1))
                v, a, e, l = (fg[:, i, :] for i in range(4))
                act.activation(a, v, ACT.Abs).then_inc(act_step, 1)
                act.wait_ge(act_step, count_step())
                act.activation(e, a, ACT.Exp, scale=-1.0).then_inc(act_step, 1)
                act.wait_ge(act_step, count_step())
                act.activation(l, e, ACT.Ln, bias=1.0).then_inc(forget_ln, 1)

            def lambda_sums(layer):
                act.wait_ge(lam_sum, nth(lam_sum, layer, "sum"))
                act.activation(lam_e, lam_s, ACT.Exp).then_inc(lam_exp, 1)

            def qk_evac(layer, which):
                for t in range(TT):
                    act.wait_ge(stage_done, nth(stage_done, layer, ("tr_qk", which, t)))
                    act.activation(
                        qT[which][0][:, :, t * P:(t + 1) * P], bank[QK_BANKS[which][t]].rearrange("p (h q) -> p h q", h=4),
                        ACT.Copy, scale=HD ** -0.5 if which == "dq" else 1.0).then_inc(qkT_hi, 1)

            def pool_evac_a(layer):
                act.wait_ge(stage_done, nth(stage_done, layer, ("pool_a",)))
                act.activation(pooledT, bank["O"], ACT.Copy).then_inc(pooled, 1)

            def pool_evac_b(layer):
                act.wait_ge(stage_done, nth(stage_done, layer, ("pool_b",)))
                for pr in range(2):
                    lhs_part(layer, ("pool", pr), oT[0][:, pr, :], bank["T"][:, pr * SEQ:(pr + 1) * SEQ], psc[:, pr:pr + 1])

            def ss(layer):
                act.wait_ge(y_ready["attn"], nth(y_ready["attn"], layer, "y"))
                for t in range(TT):
                    wait_item(act, layer, "ss", t)
                    src = item_bank(layer, ITEM_AT["ss"], t)
                    act.activation(scratch(t, SQ), src, ACT.Copy, scale=y_attn[:, t:t + 1]).then_inc(ss_staged, 1)

            def ss_evac(layer):
                for t in range(TT):
                    act.wait_ge(stage_done, nth(stage_done, layer, ("tr_ss", t)))
                    src = bank["TO"[t]].rearrange("p (k q) -> p k q", k=4)
                    act.activation(sT[0][:, 0:2, t * P:(t + 1) * P], src[:, 0:2, :], ACT.Copy, scale=HD ** -0.5)
                    act.activation(sT[0][:, 2:4, t * P:(t + 1) * P], src[:, 2:4, :], ACT.Copy).then_inc(sT_hi, 1)

            def dv(layer):
                for t in range(TT):
                    wait_item(act, layer, "dv", t)
                    act.activation(v_d[:, t, :], item_bank(layer, ITEM_AT["dv"], t), ACT.Copy, scale=y_attn[:, t:t + 1]) \
                        .then_inc(v_ready, 1)

            def pf(layer):
                for t in range(TT):
                    act.wait_ge(forget_in, nth(forget_in, layer, t))
                    act.activation(pool_u[t], item_bank(layer, ITEM_AT["pf"], t)[:, 0:256], ACT.Copy,
                                   scale=y_attn[:, t:t + 1]).then_inc(u_ready, 1)

            def sb_logs(layer, pair):
                act.wait_ge(stage_done, nth(stage_done, layer, ("sb_scores", pair)))
                act.activation(sb1[:, :, :], bankAB[:, :, 0:384], ACT.Abs).then_inc(act_step, 1)
                act.wait_ge(act_step, count_step())
                act.activation(sb2[:, :, :], sb1[:, :, :], ACT.Exp, scale=-1.0).then_inc(act_step, 1)
                act.wait_ge(act_step, count_step())
                act.activation(sb1[:, :, :], sb2[:, :, :], ACT.Ln, bias=1.0).then_inc(sb_ln, 1)

            def sb_split(layer, pair):
                act.wait_ge(sb_sp, nth(sb_sp, layer, pair))
                act.activation(softplus[0][:, :, :], sb2[:, :, :], ACT.Copy).then_inc(sb_hi, 1)

            def sb_weights(layer, pair):
                act.wait_ge(stage_done, nth(stage_done, layer, ("sb_sums", pair)))
                act.activation(sb1[:, :, :], bankAB[:, :, 0:384], ACT.Exp).then_inc(sb_w, 1)

            def sb_evac(layer, pair):
                act.wait_ge(stage_done, nth(stage_done, layer, ("sb_out", pair)))
                lhs_part(layer, ("sb", pair), oT[0][:, 6 + pair, :], bank["O"][:, 0:SEQ])

            def svfq(layer):
                act.wait_ge(normed, nth(normed, layer, ("dk", 1)))
                head_squares(layer, "fq", "svfq", 256, 256, v_s)

            def fkfv(layer):
                act.wait_ge(normed, nth(normed, layer, ("fq", 1)))
                head_squares(layer, "fk", "fkfv", 0, 256, v_f)

            def fox_evac(layer, which):
                for t in range(TT):
                    act.wait_ge(stage_done, nth(stage_done, layer, ("tr_fox", which, t)))
                    act.activation(
                        qT[which][0][0:HD + 2, :, t * P:(t + 1) * P], bank["AB"[t]][0:HD + 2, :].rearrange("p (h q) -> p h q", h=4),
                        ACT.Copy).then_inc(qkT_hi, 1)

            def softmax(layer, kind, h):
                act.wait_ge(maxed, nth(maxed, layer, (kind, h)))
                if (kind, h) != jobs[0]:
                    act.wait_ge(probs_ready, nth(probs_ready, layer, jobs[jobs.index((kind, h)) - 1]))
                maps = [("A", 0), ("B", 1)] if kind == "diff" else [("AB"[h % 2], 0)]
                for b, m in maps:
                    act.activation(expd[:, m, 0:256], bank[b][:, 0:256], ACT.Exp, bias=nmx[:, m:m + 1],
                                   accum_out=den[:, m:m + 1])
                    last = act.activation(expd[:, m, 256:384], bank[b][:, 256:384], ACT.Exp, bias=nmx[:, 2 + m:3 + m],
                                          accum_out=den[:, 2 + m:3 + m])
                last.then_inc(exped, 1)

            def probs_evac(layer, kind, h):
                act.wait_ge(stage_done, nth(stage_done, layer, ("tr_probs", kind, h)))
                act.activation(probsT[:, :], bank["T"][:, 0:384], ACT.Copy).then_inc(probsT_ready, 1)

            def pv_evac(layer, kind, h):
                if kind == "fox":
                    act.wait_ge(stage_done, nth(stage_done, layer, ("pv", kind, h)))
                    r = (h % 2) * HD
                    lhs_part(layer, ("fox", h), oT[0][r:r + HD, 8 + h // 2, :], bank["O"][r:r + HD, 0:SEQ])

            def diff_evac(layer, t):
                act.wait_ge(stage_done, nth(stage_done, layer, ("tr_diff", t)))
                lhs_part(layer, ("diff", t), oT[0][:, 2:6, t * P:(t + 1) * P],
                         bank["TO"[t]].rearrange("p (h q) -> p h q", h=4), gsub)

            def sigmoid(layer, n, t):
                act.wait_ge(gate_ready, nth(gate_ready, layer, (2 * n + 1, t)))
                g = wide[:, t, n * D:(n + 1) * D]
                act.activation(g, g, ACT.Sigmoid).then_inc(gate_open, 1)

            def merged_evac(layer, j):
                for t in range(TT):
                    act.wait_ge(stage_done, nth(stage_done, layer, ("tr_merged", j, t)))
                    lhs_part(layer, ("merged", j, t), hT[0][:, 4 * j:4 * j + 4, t * P:(t + 1) * P],
                             bank[("AB", "TO")[j][t]].rearrange("p (k q) -> p k q", k=4))

            def ff_gate(layer, p):
                item, width = (("ffg", p), NC) if p < NPAIR else ("fflast", 256)
                if p == 0:
                    act.wait_ge(y_ready["ffn"], nth(y_ready["ffn"], layer, "y"))
                for t in range(TT):
                    wait_item(act, layer, item, t)
                    if p >= 2:
                        act.wait_ge(ff_ready, nth(ff_ready, layer, (p - 2, t)))
                    act.activation(ff_tmp(t, p, width), item_bank(layer, ITEM_AT[item], t)[:, 0:width],
                                   ACT.Sigmoid, scale=y_ffn[:, t:t + 1]).then_inc(ff_sig, 1)

            def act_evac(layer, p):
                blocks = 4 if p < NPAIR else 2
                for t in range(TT):
                    act.wait_ge(stage_done, nth(stage_done, layer, ("tr_act", p, t)))
                    lhs_part(layer, ("act", p, t), aT[0][:, 4 * p:4 * p + blocks, t * P:(t + 1) * P],
                             bank[("AB", "TO")[p % 2][t]][:, 0:blocks * P].rearrange("p (k q) -> p k q", k=blocks))

            def nothing(*_):
                pass

            stages = dict(residual=nothing, gain=nothing, squares=row_squares, norm_ffn=nothing, norm_evac=norm_evac,
                          qk_norm=qk_norm, lambda_sums=lambda_sums, lambdas=nothing, pf=pf, sb_split=sb_split, maxima=nothing,
                          fox_forget=fox_forget, qk_evac=qk_evac, cum_evac=nothing, pool_evac_a=pool_evac_a,
                          pool_evac_b=pool_evac_b, ss=ss, ss_evac=ss_evac, sb_logs=sb_logs, svfq=svfq,
                          sb_weights=sb_weights, sb_evac=sb_evac, fox_evac=fox_evac, fkfv=fkfv, dv=dv,
                          softmax=softmax, probs_evac=probs_evac, pv_evac=pv_evac, diff_norm=nothing,
                          diff_evac=diff_evac, gate=nothing, sigmoid=sigmoid, branch=nothing,
                          merged_evac=merged_evac, ff_gate=ff_gate, ff_up=nothing, act_evac=act_evac)
            split_hi(0)
            for b in range(2):
                norm_evac(0, "attn", 0, b)
            split_hi(1)
            split_hi(2)
            for b in range(2):
                norm_evac(0, "attn", 1, b)
            for g in range(3, AHEAD):
                split_hi(g)
            for g in range(DEPTH * U):
                layer, u = divmod(g, U)
                for stage, *args in SV_TIMETABLE.get(u, ()):
                    if g < 2 and stage in ("norm_evac", "gain"):
                        continue
                    stages[stage](layer, *args)
                if u == 2:
                    act.preload_act_table_set("natural_log_exp_and_others")
                if g + AHEAD < DEPTH * U:
                    split_hi(g + AHEAD)

        @block.vector
        def _(vec):
            steps = [0]

            def count_step():
                steps[0] += 1
                return steps[0]

            def split_lo(g):
                layer, u = divmod(g, U)
                width = sum(w for _, w in ITEMS[UNITS[u][0]][2])
                vec.wait_ge(hi_ready, nth(hi_ready, layer, u))
                vec.tensor_tensor(w_lo[:, g % RING, :, 0:width], raw[:, g % RAW, :, 0:width],
                                  w_hi[:, g % RING, :, 0:width].bitcast(F32), ALU.subtract).then_inc(lo_ready, 1)

            def lhs_rest(layer, event, dst, src, high, scale=None):
                vec.wait_ge(lhs_hi, nth(lhs_hi, layer, event))
                if scale is None:
                    ins = vec.tensor_tensor(dst, src, high.bitcast(F32), ALU.subtract)
                else:
                    ins = vec.scalar_tensor_tensor(out=dst, in0=src, scalar=scale, in1=high.bitcast(F32),
                                                   op0=ALU.mult, op1=ALU.subtract)
                ins.then_inc(lhs_lo, 1)

            m_, h_, y_, a_ = (stat[:, 20 * i:20 * i + 20] for i in range(4))

            def rsqrt(n):
                m, h, y, a = m_[:, 0:n], h_[:, 0:n], y_[:, 0:n], a_[:, 0:n]
                vec.tensor_scalar(h, m, -0.5, None, ALU.mult)
                vec.tensor_scalar(y.bitcast(I32), m.bitcast(I32), -0.5, RSQRT_MAGIC, ALU.mult, ALU.add).then_inc(vec_step, 1)
                vec.wait_ge(vec_step, count_step())
                for _ in range(3):
                    vec.tensor_tensor(a, y, y, ALU.mult).then_inc(vec_step, 1)
                    vec.wait_ge(vec_step, count_step())
                    vec.tensor_tensor(a, a, h, ALU.mult).then_inc(vec_step, 1)
                    vec.wait_ge(vec_step, count_step())
                    vec.scalar_tensor_tensor(out=y, in0=a, scalar=1.5, in1=y, op0=ALU.add, op1=ALU.mult) \
                        .then_inc(vec_step, 1)
                    vec.wait_ge(vec_step, count_step())

            def mean_square(which, layer, n):
                vec.wait_ge(sumsq[which], nth(sumsq[which], layer, (1, 1)))
                vec.tensor_tensor(m_[:, n:n + TT], ssq[:, :, 0], ssq[:, :, 1], ALU.add).then_inc(vec_step, 1)
                vec.wait_ge(vec_step, count_step())
                vec.tensor_scalar(m_[:, n:n + TT], m_[:, n:n + TT], 1.0 / D, EPS, ALU.mult, ALU.add).then_inc(vec_step, 1)
                vec.wait_ge(vec_step, count_step())

            def residual(layer, which, t, j):
                if layer < 0:
                    return
                wait_item(vec, layer, (which, j), t)
                xs = x_sb[:, t, j * NC:(j + 1) * NC]
                vec.tensor_tensor(xs, item_bank(layer, ITEM_AT[(which, j)], t), xs, ALU.add) \
                    .then_inc(x_out if which == "out" else x_down, 1)

            def gain(layer, which, t, j):
                if layer == DEPTH:
                    return
                half = slice(j * NC, (j + 1) * NC)
                if which == "ffn":
                    vec.wait_ge(x_out, nth(x_out, layer, (t, j)))
                elif layer:
                    vec.wait_ge(x_down, nth(x_down, layer - 1, (t, j)))
                else:
                    vec.wait_ge(x_loaded[t], 16)
                vec.wait_ge(gain_loaded[which], 16 * (layer + 1))
                vec.tensor_tensor(hn(t)[:, half], x_sb[:, t, half], gain_row[which][:, half], ALU.mult) \
                    .then_inc(hn_ready[which], 1)

            def norm_ffn(layer):
                mean_square("ffn", layer, 0)
                rsqrt(TT)
                vec.tensor_copy(y_ffn[:, :], y_[:, 0:TT]).then_inc(y_ready["ffn"], 1)
                vec.wait_ge(y_ready["ffn"], nth(y_ready["ffn"], layer, "y"))

            def norm_evac(layer, which, t, b):
                lhs_rest(layer, ("norm", which, t, b), hT[1][:, 4 * b:4 * b + 4, t * P:(t + 1) * P],
                         bank["ABTO"[2 * t + b]].rearrange("p (k q) -> p k q", k=4),
                         hT[0][:, 4 * b:4 * b + 4, t * P:(t + 1) * P])

            def head_norm(layer, which, item, c0, heads):
                width, n = heads * HD, TT * heads
                if which == "dq":
                    mean_square("attn", layer, n)
                    vec.tensor_scalar(eps_heads[:, :], m_[:, n:n + TT], EPS, None, ALU.mult)
                for t in range(TT):
                    vec.wait_ge(squares, nth(squares, layer, (which, t)))
                    last = vec.reduce_sum(m_[:, t * heads:(t + 1) * heads],
                                          scratch(t, SQ, width).rearrange("p (h d) -> p h d", d=HD), AX_X)
                last.then_inc(vec_step, 1)
                vec.wait_ge(vec_step, count_step())
                for t in range(TT):
                    m = m_[:, t * heads:(t + 1) * heads]
                    last = vec.tensor_scalar(m, m, 1.0 / HD, eps_heads[:, t:t + 1], ALU.mult, ALU.add)
                last.then_inc(vec_step, 1)
                vec.wait_ge(vec_step, count_step())
                rsqrt(n + TT if which == "dq" else n)
                for t in range(TT):
                    src = item_bank(layer, ITEM_AT[item], t)[:, c0:c0 + width].rearrange("p (h d) -> p h d", d=HD)
                    vec.tensor_tensor(xn(which, t).rearrange("p (h d) -> p h d", d=HD), src,
                                      y_[:, t * heads:(t + 1) * heads].unsqueeze(2).broadcast_to([P, heads, HD]),
                                      ALU.mult).then_inc(normed, 1)
                if which == "dq":
                    vec.tensor_copy(y_attn[:, :], y_[:, n:n + TT]).then_inc(y_ready["attn"], 1)
                    vec.wait_ge(y_ready["attn"], nth(y_ready["attn"], layer, "y"))

            def qk_norm(layer, which):
                head_norm(layer, which, which, 0, 8)

            def pf_items(layer):
                for t in range(TT):
                    wait_item(vec, layer, "pf", t)
                    src = item_bank(layer, ITEM_AT["pf"], t)
                    vec.scalar_tensor_tensor(out=fg[:, 4, 4 * t:4 * t + 4], in0=src[:, 256:260], scalar=y_attn[:, t:t + 1], in1=b_f,
                                             op0=ALU.mult, op1=ALU.add).then_inc(vec_step, 1)
                    vec.wait_ge(vec_step, count_step())
                    vec.tensor_scalar(fg[:, 0, 4 * t:4 * t + 4], fg[:, 4, 4 * t:4 * t + 4], -1.0, None, ALU.mult) \
                        .then_inc(forget_in, 1)

            def lambda_sums(layer):
                vec.wait_ge(params_loaded, 16 * PARAM_DMAS * (layer + 1))
                tmp = wide[:, 0, 1280:1408].rearrange("p (i d) -> p i d", i=2)
                lv = lamv[:, :, :].rearrange("p (i two) d -> p i two d", two=2)
                vec.tensor_tensor(tmp, lv[:, :, 0, :], lv[:, :, 1, :], ALU.mult).then_inc(vec_step, 1)
                vec.wait_ge(vec_step, count_step())
                vec.reduce_sum(lam_s, tmp, AX_X).then_inc(lam_sum, 1)

            def fox_forget(layer):
                vec.wait_ge(forget_ln, nth(forget_ln, layer, "ln"))
                vec.scalar_tensor_tensor(out=fg[:, 4, :], in0=fg[:, 0, :], scalar=0.0, in1=fg[:, 3, :],
                                         op0=ALU.max, op1=ALU.add).then_inc(forget_out, 1)

            def lambdas(layer):
                vec.wait_ge(lam_exp, nth(lam_exp, layer, "exp"))
                vec.tensor_tensor(neglam, lam_e[:, 1:2], lam_e[:, 0:1], ALU.subtract).then_inc(vec_step, 1)
                vec.wait_ge(vec_step, count_step())
                vec.tensor_tensor(neglam, neglam, c("lam")[:, layer:layer + 1], ALU.subtract).then_inc(lam_sum, 1)
                vec.tensor_tensor(gsub, subln, c("one_minus_lam")[:, layer:layer + 1], ALU.mult).then_inc(vec_step, 1)
                vec.wait_ge(vec_step, count_step())

            def cum_evac(layer):
                vec.wait_ge(stage_done, nth(stage_done, layer, ("cum",)))
                cumulated = bank["T"][:, 0:8].rearrange("p (t h) -> p t h", t=TT)
                vec.tensor_scalar(aug["fk"][:, :, :, HD], cumulated, -1.0, None, ALU.mult)
                vec.tensor_copy(aug["fq"][:, :, :, HD + 1], cumulated).then_inc(forget_out, 1)

            def pool_evac_b(layer):
                vec.wait_ge(lhs_hi, nth(lhs_hi, layer, ("pool", 1)))
                for pr in range(2):
                    lhs_rest(layer, ("pool", pr), oT[1][:, pr, :], bank["T"][:, pr * SEQ:(pr + 1) * SEQ], oT[0][:, pr, :],
                             psc[:, pr:pr + 1])

            def sb_logs(layer, pair):
                vec.wait_ge(sb_ln, nth(sb_ln, layer, pair))
                vec.scalar_tensor_tensor(out=sb2[:, :, :], in0=bankAB[:, :, 0:384], scalar=0.0, in1=sb1[:, :, :],
                                         op0=ALU.max, op1=ALU.add).then_inc(vec_step, 1)
                vec.wait_ge(vec_step, count_step())
                vec.tensor_tensor(sb2[:, :, 0:128], sb2[:, :, 0:128],
                                  c("strict").unsqueeze(1).broadcast_to([P, 2, P]), ALU.mult)
                vec.tensor_tensor(sb2[:, :, 256:384], sb2[:, :, 256:384],
                                  c("strict").unsqueeze(1).broadcast_to([P, 2, P]), ALU.mult).then_inc(sb_sp, 1)

            def sb_split(layer, pair):
                vec.wait_ge(sb_hi, nth(sb_hi, layer, pair))
                vec.tensor_tensor(softplus[1][:, :, :], sb2[:, :, :], softplus[0][:, :, :].bitcast(F32), ALU.subtract) \
                    .then_inc(sb_lo, 1)

            def qk_evac(layer, which):
                for t in range(TT):
                    vec.wait_ge(qkT_hi, nth(qkT_hi, layer, (which, t)))
                    high, low = (part[:, :, t * P:(t + 1) * P] for part in qT[which])
                    vec.scalar_tensor_tensor(out=low, in0=bank[QK_BANKS[which][t]].rearrange("p (h q) -> p h q", h=4),
                                             scalar=HD ** -0.5 if which == "dq" else 1.0, in1=high.bitcast(F32),
                                             op0=ALU.mult, op1=ALU.subtract).then_inc(qkT_ready, 1)

            def fox_evac(layer, which):
                for t in range(TT):
                    vec.wait_ge(qkT_hi, nth(qkT_hi, layer, (which, t)))
                    high, low = (part[0:HD + 2, :, t * P:(t + 1) * P] for part in qT[which])
                    vec.tensor_tensor(low, bank["AB"[t]][0:HD + 2, :].rearrange("p (h q) -> p h q", h=4), high.bitcast(F32),
                                      ALU.subtract).then_inc(qkT_ready, 1)

            def ss_evac(layer):
                for t in range(TT):
                    vec.wait_ge(sT_hi, nth(sT_hi, layer, t))
                    src = bank["TO"[t]].rearrange("p (k q) -> p k q", k=4)
                    high, low = (part[:, :, t * P:(t + 1) * P] for part in sT)
                    vec.scalar_tensor_tensor(out=low[:, 0:2, :], in0=src[:, 0:2, :], scalar=HD ** -0.5,
                                             in1=high[:, 0:2, :].bitcast(F32), op0=ALU.mult, op1=ALU.subtract)
                    vec.tensor_tensor(low[:, 2:4, :], src[:, 2:4, :], high[:, 2:4, :].bitcast(F32),
                                      ALU.subtract).then_inc(sT_ready, 1)

            def sb_evac(layer, pair):
                lhs_rest(layer, ("sb", pair), oT[1][:, 6 + pair, :], bank["O"][:, 0:SEQ], oT[0][:, 6 + pair, :])

            def svfq(layer):
                head_norm(layer, "fq", "svfq", 256, 4)

            def fkfv(layer):
                head_norm(layer, "fk", "fkfv", 0, 4)

            def maxima(layer, kind, h):
                vec.wait_ge(stage_done, nth(stage_done, layer, ("scores", kind, h)))
                mx = row_max[:, :]
                if kind == "diff":
                    vec.reduce_max(mx[:, 0:2], bankAB[:, :, 0:256], AX_X)
                    vec.reduce_max(mx[:, 2:4], bankAB[:, :, 256:384], AX_X).then_inc(vec_step, 1)
                    vec.wait_ge(vec_step, count_step())
                    vec.tensor_scalar(nmx[:, :], mx, -1.0, None, ALU.mult).then_inc(maxed, 1)
                else:
                    b = bank["AB"[h % 2]]
                    vec.reduce_max(mx[:, 0:1], b[:, 0:256], AX_X)
                    vec.reduce_max(mx[:, 2:3], b[:, 256:384], AX_X).then_inc(vec_step, 1)
                    vec.wait_ge(vec_step, count_step())
                    vec.tensor_scalar(nmx[:, 0:3:2], mx[:, 0:3:2], -1.0, None, ALU.mult).then_inc(maxed, 1)

            def softmax(layer, kind, h):
                vec.wait_ge(exped, nth(exped, layer, (kind, h)))
                if (kind, h) != jobs[0]:
                    before = jobs[jobs.index((kind, h)) - 1]
                    vec.wait_ge(stage_done, nth(stage_done, layer, ("tr_probs", *before)))
                r = inverse[:, :]
                if kind == "diff":
                    vec.reciprocal(r, den[:, :]).then_inc(vec_step, 1)
                    vec.wait_ge(vec_step, count_step())
                    vec.tensor_scalar(r[:, 1:4:2], r[:, 1:4:2], neglam, None, ALU.mult).then_inc(vec_step, 1)
                    vec.wait_ge(vec_step, count_step())
                    vec.tensor_scalar(probs[:, 0:256], expd[:, 0, 0:256], r[:, 0:1], None, ALU.mult)
                    vec.tensor_scalar(probs[:, 256:384], expd[:, 0, 256:384], r[:, 2:3], None, ALU.mult) \
                        .then_inc(vec_step, 1)
                    vec.wait_ge(vec_step, count_step())
                    vec.scalar_tensor_tensor(out=probs[:, 0:256], in0=expd[:, 1, 0:256], scalar=r[:, 1:2],
                                             in1=probs[:, 0:256], op0=ALU.mult, op1=ALU.add)
                    last = vec.scalar_tensor_tensor(out=probs[:, 256:384], in0=expd[:, 1, 256:384], scalar=r[:, 3:4],
                                                    in1=probs[:, 256:384], op0=ALU.mult, op1=ALU.add)
                else:
                    vec.reciprocal(r[:, 0:3:2], den[:, 0:3:2]).then_inc(vec_step, 1)
                    vec.wait_ge(vec_step, count_step())
                    vec.tensor_scalar(probs[:, 0:256], expd[:, 0, 0:256], r[:, 0:1], None, ALU.mult)
                    last = vec.tensor_scalar(probs[:, 256:384], expd[:, 0, 256:384], r[:, 2:3], None, ALU.mult)
                last.then_inc(probs_ready, 1)

            def pv_evac(layer, kind, h):
                if kind == "diff":
                    vec.wait_ge(stage_done, nth(stage_done, layer, ("pv", kind, h)))
                    vec.tensor_copy(o_d[:, :, h, :], bank["O"][:, 0:SEQ].rearrange("p (t d) -> p t d", t=TT)) \
                        .then_inc(o_d_ready, 1)
                else:
                    r = (h % 2) * HD
                    lhs_rest(layer, ("fox", h), oT[1][r:r + HD, 8 + h // 2, :], bank["O"][r:r + HD, 0:SEQ],
                             oT[0][r:r + HD, 8 + h // 2, :])

            def diff_norm(layer):
                vec.wait_ge(o_sq, nth(o_sq, layer, "squares"))
                for t in range(TT):
                    ins = vec.reduce_sum(m_[:, 4 * t:4 * t + 4], scratch(t, TB).rearrange("p (h d) -> p h d", h=4), AX_X)
                ins.then_inc(vec_step, 1)
                vec.wait_ge(vec_step, count_step())
                vec.tensor_scalar(m_[:, 0:8], m_[:, 0:8], 1.0 / P, EPS, ALU.mult, ALU.add).then_inc(vec_step, 1)
                vec.wait_ge(vec_step, count_step())
                rsqrt(8)
                for t in range(TT):
                    last = vec.tensor_tensor(o_d[:, t, :, :], o_d[:, t, :, :],
                                             y_[:, 4 * t:4 * t + 4].unsqueeze(2).broadcast_to([P, 4, P]), ALU.mult)
                last.then_inc(o_normed, 1)

            def diff_evac(layer, t):
                lhs_rest(layer, ("diff", t), oT[1][:, 2:6, t * P:(t + 1) * P],
                         bank["TO"[t]].rearrange("p (h q) -> p h q", h=4), oT[0][:, 2:6, t * P:(t + 1) * P], gsub)

            def gate(layer, g):
                if g == 1:
                    vec.wait_ge(rotated, nth(rotated, layer, ("fk", 1)))
                for t in range(TT):
                    wait_item(vec, layer, ("gate", g), t)
                    vec.wait_ge(bias_loaded[g % 2], 16 * (4 * layer + g // 2 + 1))
                    vec.scalar_tensor_tensor(out=wide[:, t, g * NC:(g + 1) * NC], in0=item_bank(layer, ITEM_AT[("gate", g)], t),
                                             scalar=y_attn[:, t:t + 1], in1=bias[:, g % 2, :], op0=ALU.mult,
                                             op1=ALU.add).then_inc(gate_ready, 1)

            def branch(layer, j, n):
                for t in range(TT):
                    wait_item(vec, layer, ("branch", j, n), t)
                    vec.wait_ge(gate_open, nth(gate_open, layer, (n, t)))
                    g = wide[:, t, n * D + j * NC:n * D + (j + 1) * NC]
                    vec.tensor_tensor(g, item_bank(layer, ITEM_AT[("branch", j, n)], t), g, ALU.mult).then_inc(gated, 1)

            def merged_evac(layer, j):
                for t in range(TT):
                    lhs_rest(layer, ("merged", j, t), hT[1][:, 4 * j:4 * j + 4, t * P:(t + 1) * P],
                             bank[("AB", "TO")[j][t]].rearrange("p (k q) -> p k q", k=4),
                             hT[0][:, 4 * j:4 * j + 4, t * P:(t + 1) * P])

            def ff_gate(layer, p):
                item, width = (("ffg", p), NC) if p < NPAIR else ("fflast", 256)
                for t in range(TT):
                    vec.wait_ge(ff_sig, nth(ff_sig, layer, (p, t)))
                    s = ff_tmp(t, p, width)
                    vec.scalar_tensor_tensor(out=s, in0=item_bank(layer, ITEM_AT[item], t)[:, 0:width], scalar=y_ffn[:, t:t + 1],
                                             in1=s, op0=ALU.mult, op1=ALU.mult).then_inc(ff_gated, 1)

            def ff_up(layer, p):
                item, c0, width = (("ffu", p), 0, NC) if p < NPAIR else ("fflast", 256, 256)
                for t in range(TT):
                    wait_item(vec, layer, item, t)
                    vec.wait_ge(ff_gated, nth(ff_gated, layer, (p, t)))
                    if p >= 2:
                        vec.wait_ge(stage_done, nth(stage_done, layer, ("tr_act", p - 2, t)))
                    vec.scalar_tensor_tensor(out=ff_act(t, p, width), in0=item_bank(layer, ITEM_AT[item], t)[:, c0:c0 + width],
                                             scalar=y_ffn[:, t:t + 1], in1=ff_tmp(t, p, width), op0=ALU.mult,
                                             op1=ALU.mult).then_inc(ff_ready, 1)

            def act_evac(layer, p):
                blocks = 4 if p < NPAIR else 2
                for t in range(TT):
                    dst = slice(4 * p, 4 * p + blocks)
                    lhs_rest(layer, ("act", p, t), aT[1][:, dst, t * P:(t + 1) * P],
                             bank[("AB", "TO")[p % 2][t]][:, 0:blocks * P].rearrange("p (k q) -> p k q", k=blocks),
                             aT[0][:, dst, t * P:(t + 1) * P])

            def nothing(*_):
                pass

            stages = dict(residual=residual, gain=gain, squares=nothing, norm_ffn=norm_ffn, norm_evac=norm_evac,
                          qk_norm=qk_norm, lambda_sums=lambda_sums, lambdas=lambdas, pf=pf_items, sb_split=sb_split, maxima=maxima,
                          fox_forget=fox_forget, qk_evac=qk_evac, cum_evac=cum_evac, pool_evac_a=nothing,
                          pool_evac_b=pool_evac_b, ss=nothing, ss_evac=ss_evac, sb_logs=sb_logs, svfq=svfq,
                          sb_weights=nothing, sb_evac=sb_evac, fox_evac=fox_evac, fkfv=fkfv, dv=nothing,
                          softmax=softmax, probs_evac=nothing, pv_evac=pv_evac, diff_norm=diff_norm,
                          diff_evac=diff_evac, gate=gate, sigmoid=nothing, branch=branch,
                          merged_evac=merged_evac, ff_gate=ff_gate, ff_up=ff_up, act_evac=act_evac)

            vec.memset(warm[:, :], 0.0).then_inc(warm_ready, 1)
            for j in range(2):
                gain(0, "attn", 0, j)
            split_lo(0)
            for b in range(2):
                norm_evac(0, "attn", 0, b)
            split_lo(1)
            for j in range(2):
                gain(0, "attn", 1, j)
            split_lo(2)
            for b in range(2):
                norm_evac(0, "attn", 1, b)
            for g in range(3, AHEAD):
                split_lo(g)
            for g in range(DEPTH * U):
                layer, u = divmod(g, U)
                if g == FIRST["dk"]:
                    vec.wait_ge(consts_loaded, 16)
                    for i, name in enumerate(("ident", "causal", "strict_neg")):
                        vec.tensor_copy(masks[:, i, :], c(name))
                    for i, name in enumerate(("minus_from", "minus_ones")):
                        last = vec.tensor_copy(sums[:, i, :], c(name))
                    last.then_inc(masks_ready, 1)
                for stage, *args in SV_TIMETABLE.get(u, ()):
                    if g < 2 and stage in ("norm_evac", "gain"):
                        continue
                    ahead = stage == "gain" and args[0] == "attn" and u > F0
                    behind = stage == "residual" and args[0] == "down" and u == 0
                    stages[stage](layer + ahead - behind, *args)
                if g + AHEAD < DEPTH * U:
                    split_lo(g + AHEAD)
            residual(DEPTH - 1, "down", 1, 1)

        @block.tensor
        def _(pe):
            identity = c("ident")
            last_read = {b: None for b in "ABTO"}

            def take(banks, *freed):
                for b in banks:
                    if last_read[b] is not None:
                        sig, layer, event = last_read[b]
                        pe.wait_ge(sig, nth(sig, layer, event))
                    last_read[b] = freed

            def product(dst, a, b, start, stop):
                pe.matmul(dst, a[0], b[0], start=start, stop=False, skip_group_check=True)
                pe.matmul(dst, a[0], b[1], start=False, stop=False, skip_group_check=True)
                return pe.matmul(dst, a[1], b[0], start=False, stop=stop, skip_group_check=True)

            def tr_norm(layer, which, t, b):
                pe.wait_ge(hn_ready[which], nth(hn_ready[which], layer, (t, b)))
                name = "ABTO"[2 * t + b]
                take(name, lhs_lo, layer, ("norm", which, t, b))
                for k in range(4):
                    ins = pe.transpose(bank[name][:, k * P:(k + 1) * P], hn(t)[:, (4 * b + k) * P:(4 * b + k + 1) * P], identity)
                ins.then_inc(stage_done, 1)

            def tr_qk(layer, which):
                for t in range(TT):
                    pe.wait_ge(rotated, nth(rotated, layer, (which, t)))
                    name = QK_BANKS[which][t]
                    take(name, qkT_ready, layer, (which, t))
                    for k in range(4):
                        ins = pe.transpose(bank[name][:, k * P:(k + 1) * P], xn(which, t)[:, k * P:(k + 1) * P], identity)
                    ins.then_inc(stage_done, 1)

            def tr_fox(layer, which):
                pe.wait_ge(forget_out, nth(forget_out, layer, "aug"))
                for t in range(TT):
                    pe.wait_ge(rotated, nth(rotated, layer, (which, t)))
                    take("AB"[t], qkT_ready, layer, (which, t))
                    for h in range(4):
                        ins = pe.transpose(bank["AB"[t]][0:HD + 2, h * P:(h + 1) * P], aug[which][:, t, h, :], identity)
                    ins.then_inc(stage_done, 1)

            def tr_ss(layer):
                for t in range(TT):
                    pe.wait_ge(ss_staged, nth(ss_staged, layer, t))
                    take("TO"[t], sT_ready, layer, t)
                    for k in range(4):
                        ins = pe.transpose(bank["TO"[t]][:, k * P:(k + 1) * P], scratch(t, SQ)[:, k * P:(k + 1) * P], identity)
                    ins.then_inc(stage_done, 1)

            def cum(layer):
                pe.wait_ge(forget_out, nth(forget_out, layer, "softplus"))
                take("T", forget_out, layer, "aug")
                sp = fg[:, 4, :]
                pe.matmul(bank["T"][:, 0:8], c("minus_upto"), sp, start=True, stop=False, skip_group_check=True)
                ins = pe.matmul(bank["T"][:, 4:8], c("minus_ones"), sp[:, 0:4], start=False, stop=True, skip_group_check=True)
                ins.then_inc(stage_done, 1)

            def pool_a(layer):
                for t in range(TT):
                    pe.wait_ge(u_ready, nth(u_ready, layer, t))
                pe.wait_ge(bands_loaded, 16)
                take("O", pooled, layer, "pooled")
                for g in range(4):
                    r, at = (g % 2) * HD, (g // 2) * SEQ
                    pe.matmul(bank["O"][r:r + HD, at:at + SEQ], pool_u[0][:, g * HD:(g + 1) * HD], c(f"band0_{g}"),
                              start=(g < 2), stop=False, skip_group_check=True)
                    ins = pe.matmul(bank["O"][r:r + HD, at + P:at + SEQ], pool_u[1][:, g * HD:(g + 1) * HD], c(f"band1_{g}"),
                                    start=False, stop=True, skip_group_check=True)
                ins.then_inc(stage_done, 1)

            def pool_b(layer):
                pe.wait_ge(pooled, nth(pooled, layer, "pooled"))
                take("T", lhs_lo, layer, ("pool", 1))
                for pr in range(2):
                    ins = pe.matmul(bank["T"][:, pr * SEQ:(pr + 1) * SEQ], poolw[:, pr, :], pooledT[:, pr * SEQ:(pr + 1) * SEQ],
                                    start=(pr == 0), stop=True, skip_group_check=True)
                ins.then_inc(stage_done, 1)

            def sb_scores(layer, pair):
                for t in range(TT):
                    pe.wait_ge(sT_ready, nth(sT_ready, layer, t))
                take("AB", sb_w, layer, pair)
                for i in range(2):
                    r = slice(i * HD, (i + 1) * HD)
                    b = bank["AB"[i]]
                    product(b[:, 0:SEQ], [part[r, 2 + pair, 0:P] for part in sT], [part[r, pair, :] for part in sT], True, True)
                    ins = product(b[:, SEQ:SEQ + P], [part[r, 2 + pair, P:SEQ] for part in sT],
                                  [part[r, pair, P:SEQ] for part in sT], False, True)
                ins.then_inc(stage_done, 1)

            def sb_sums(layer, pair):
                pe.wait_ge(masks_ready, 1)
                pe.wait_ge(sb_lo, nth(sb_lo, layer, pair))
                for i in range(2):
                    b = bank["AB"[i]]
                    for part in softplus:
                        sp = part[:, i, :]
                        pe.matmul(b[:, 0:SEQ], sums[:, 0, :], sp[:, 0:SEQ], start=False, stop=False, skip_group_check=True)
                        pe.matmul(b[:, P:SEQ], sums[:, 1, :], sp[:, SEQ:SEQ + P], start=False, stop=False, skip_group_check=True)
                        pe.matmul(b[:, SEQ:SEQ + P], sums[:, 0, :], sp[:, SEQ:SEQ + P], start=False, stop=False,
                                  skip_group_check=True)
                    pe.matmul(b[:, 0:P], masks[:, 0, :], masks[:, 2, :], start=False, stop=False, skip_group_check=True)
                    ins = pe.matmul(b[:, SEQ:SEQ + P], masks[:, 0, :], masks[:, 2, :], start=False, stop=True, skip_group_check=True)
                ins.then_inc(stage_done, 1)

            def sb_out(layer, pair):
                pe.wait_ge(sb_w, nth(sb_w, layer, pair))
                pe.wait_ge(v_ready, nth(v_ready, layer, ("sv", 1)))
                take("O", lhs_lo, layer, ("sb", pair))
                for i in range(2):
                    r, h = i * HD, 2 * pair + i
                    pe.matmul(bank["O"][r:r + HD, 0:SEQ], v_s[:, 0, h * HD:(h + 1) * HD], sb1[:, i, 0:SEQ],
                              start=True, stop=False, skip_group_check=True)
                    ins = pe.matmul(bank["O"][r:r + HD, P:SEQ], v_s[:, 1, h * HD:(h + 1) * HD], sb1[:, i, SEQ:SEQ + P],
                                    start=False, stop=True, skip_group_check=True)
                ins.then_inc(stage_done, 1)

            def scores(layer, kind, h):
                pe.wait_ge(masks_ready, 1)
                q, k = ("dq", "dk") if kind == "diff" else ("fq", "fk")
                for w in (q, k):
                    for t in range(TT):
                        pe.wait_ge(qkT_ready, nth(qkT_ready, layer, (w, t)))
                banks = "AB" if kind == "diff" else "AB"[h % 2]
                take(banks, exped, layer, (kind, h))
                for i, name in enumerate(banks):
                    r = slice(i * HD, (i + 1) * HD) if kind == "diff" else slice(0, HD + 2)
                    b = bank[name]
                    product(b[:, 0:SEQ], [part[r, h, P:SEQ] for part in qT[q]], [part[r, h, :] for part in qT[k]], True, False)
                    product(b[:, SEQ:SEQ + P], [part[r, h, 0:P] for part in qT[q]], [part[r, h, 0:P] for part in qT[k]],
                            False, False)
                    pe.matmul(b[:, P:SEQ], masks[:, 0, :], masks[:, 1, :], start=False, stop=False, skip_group_check=True)
                    ins = pe.matmul(b[:, SEQ:SEQ + P], masks[:, 0, :], masks[:, 1, :], start=False, stop=True, skip_group_check=True)
                ins.then_inc(stage_done, 1)

            def tr_probs(layer, kind, h):
                pe.wait_ge(probs_ready, nth(probs_ready, layer, (kind, h)))
                take("T", probsT_ready, layer, (kind, h))
                for dst, src in ((0, 256), (128, 0), (256, 128)):
                    ins = pe.transpose(bank["T"][:, dst:dst + P], probs[:, src:src + P], identity)
                ins.then_inc(stage_done, 1)

            def pv(layer, kind, h):
                pe.wait_ge(probsT_ready, nth(probsT_ready, layer, (kind, h)))
                if kind == "diff":
                    pe.wait_ge(v_ready, nth(v_ready, layer, ("dv", 1)))
                    take("O", o_d_ready, layer, h)
                    v = [v_d[:, t, h * P:(h + 1) * P] for t in range(TT)]
                    o = bank["O"]
                    pe.matmul(o[:, 0:P], probsT[:, 0:P], v[0], start=True, stop=False, skip_group_check=True)
                    pe.matmul(o[:, P:SEQ], probsT[:, P:SEQ], v[0], start=False, stop=False, skip_group_check=True)
                    ins = pe.matmul(o[:, P:SEQ], probsT[:, SEQ:SEQ + P], v[1], start=False, stop=True, skip_group_check=True)
                else:
                    pe.wait_ge(v_ready, nth(v_ready, layer, ("fv", 1)))
                    take("O", lhs_lo, layer, ("fox", h))
                    r = (h % 2) * HD
                    o = bank["O"][r:r + HD, :]
                    v = [v_f[:, t, h * HD:(h + 1) * HD] for t in range(TT)]
                    pe.matmul(o[:, 0:SEQ], v[0], probsT[:, 0:SEQ], start=True, stop=False, skip_group_check=True)
                    ins = pe.matmul(o[:, P:SEQ], v[1], probsT[:, SEQ:SEQ + P], start=False, stop=True, skip_group_check=True)
                ins.then_inc(stage_done, 1)

            def tr_diff(layer, t):
                pe.wait_ge(o_normed, nth(o_normed, layer, "normed"))
                take("TO"[t], lhs_lo, layer, ("diff", t))
                for h in range(4):
                    ins = pe.transpose(bank["TO"[t]][:, h * P:(h + 1) * P], o_d[:, t, h, :], identity)
                ins.then_inc(stage_done, 1)

            def tr_merged(layer, j):
                for t in range(TT):
                    pe.wait_ge(merged_ready, nth(merged_ready, layer, (j, t)))
                    name = ("AB", "TO")[j][t]
                    take(name, lhs_lo, layer, ("merged", j, t))
                    for k in range(4):
                        ins = pe.transpose(bank[name][:, k * P:(k + 1) * P], merged(t)[:, (4 * j + k) * P:(4 * j + k + 1) * P], identity)
                    ins.then_inc(stage_done, 1)

            def tr_act(layer, p):
                blocks = 4 if p < NPAIR else 2
                for t in range(TT):
                    pe.wait_ge(ff_ready, nth(ff_ready, layer, (p, t)))
                    name = ("AB", "TO")[p % 2][t]
                    take(name, lhs_lo, layer, ("act", p, t))
                    for k in range(blocks):
                        ins = pe.transpose(bank[name][:, k * P:(k + 1) * P], ff_act(t, p, blocks * P)[:, k * P:(k + 1) * P], identity)
                    ins.then_inc(stage_done, 1)

            stages = dict(tr_norm=tr_norm, tr_qk=tr_qk, tr_fox=tr_fox, tr_ss=tr_ss, cum=cum, pool_a=pool_a, pool_b=pool_b,
                          sb_scores=sb_scores, sb_sums=sb_sums, sb_out=sb_out, scores=scores, tr_probs=tr_probs, pv=pv,
                          tr_diff=tr_diff, tr_merged=tr_merged, tr_act=tr_act)

            def lhs_of(name, k, t):
                kind = name if isinstance(name, str) else name[0]
                if kind == "branch":
                    event = (("pool", k) if k < 2 else ("diff", t) if k < 6 else ("sb", k - 6) if k < 8 else ("fox", 2 * (k - 8) + 1))
                    return oT, event
                if kind == "down":
                    return aT, ("act", k // 4, t)
                if kind == "out":
                    return hT, ("merged", k // 4, t)
                which = "ffn" if kind in ("ffg", "ffu", "fflast") else "attn"
                return hT, ("norm", which, t, k // 4)

            reached = {"high": 0, "low": 0}

            def wait_high(layer, event):
                if nth(lhs_hi, layer, event) > reached["high"]:
                    reached["high"] = nth(lhs_hi, layer, event)
                    pe.wait_ge(lhs_hi, nth(lhs_hi, layer, event))

            def wait_low(layer, event):
                if nth(lhs_lo, layer, event) > reached["low"]:
                    reached["low"] = nth(lhs_lo, layer, event)
                    pe.wait_ge(lhs_lo, nth(lhs_lo, layer, event))

            def multiply(g, tiles, high=True, low=True):
                layer, u = divmod(g, U)
                n, k0 = UNITS[u]
                name, _, columns, _ = ITEMS[n]
                ks = item_k(n)
                width = sum(w for _, w in columns)
                if high and k0 == ks[0] and layer * NITEM + n >= 2:
                    before, m = divmod(layer * NITEM + n - 2, NITEM)
                    for t in tiles:
                        sig, event = released_by(ITEMS[m][0], t)
                        pe.wait_ge(sig, nth(sig, before, event))
                for i in range(2):
                    k = k0 + i
                    whi, wlo = w_hi[:, g % RING, i, 0:width], w_lo[:, g % RING, i, 0:width]
                    for t in tiles:
                        operand, event = lhs_of(name, k, t)
                        hi, lo = (part[:, k, t * P:(t + 1) * P] for part in operand)
                        dst = item_bank(layer, n, t)[:, 0:width]
                        if high:
                            if low:
                                wait_low(layer, event)
                            else:
                                wait_high(layer, event)
                            pe.matmul(dst, hi, whi, start=(k == ks[0]), stop=False)
                            pe.matmul(dst, hi, wlo, start=False, stop=False)
                        if low:
                            wait_low(layer, event)
                            ins = pe.matmul(dst, lo, whi, start=False, stop=(k == ks[-1]))
                if low and 1 in tiles:
                    ins.then_inc(unit_done, 1)
                elif low and k == ks[-1]:
                    ins.then_inc(early_done, 1)

            pe.wait_ge(warm_ready, 1)
            for _ in range(WARM_UP):
                pe.matmul(bank["O"][:, 0:P], warm[:, :], warm[:, :], start=True, stop=True)
            pe.wait_ge(identity_loaded, 16)
            tr_norm(0, *PE_NEXT[1:])
            tr_norm(0, "attn", 0, 1)
            for _ in range(WARM_UP // 5):
                pe.matmul(bank["O"][:, 0:P], warm[:, :], warm[:, :], start=True, stop=True)
            for u in range(2):
                pe.wait_ge(lo_ready, nth(lo_ready, 0, u))
                multiply(u, [0], low=False)
            for b in range(2):
                tr_norm(0, "attn", 1, b)
            for u in range(2):
                multiply(u, [0], high=False)
            for u in range(2):
                multiply(u, [1])
            pe.wait_ge(lo_ready, nth(lo_ready, 0, 2))
            multiply(2, [0, 1])
            pe.wait_ge(lo_ready, nth(lo_ready, 0, 3))
            multiply(3, [0])
            multiply(3, [1])
            for layer in range(DEPTH):
                u = 0 if layer else GROUPS[0]
                while u < U:
                    if layer == 0 and u == FIRST["dk"]:
                        pe.wait_ge(consts_loaded, 16)
                    for stage, *args in PE_TIMETABLE.get(u, ()):
                        stages[stage](layer, *args)
                    size = GROUPS.get(u, 1)
                    if size == 1:
                        pe.wait_ge(lo_ready, nth(lo_ready, layer, u))
                        multiply(layer * U + u, [0, 1])
                    else:
                        fresh = u in (0, F0)
                        for v in range(u, u + size):
                            pe.wait_ge(lo_ready, nth(lo_ready, layer, v))
                            multiply(layer * U + v, [0], low=not fresh)
                        for stage, *args in PE_MID.get(u, ()):
                            stages[stage](layer, *args)
                        if fresh:
                            for v in range(u, u + size):
                                multiply(layer * U + v, [0], high=False)
                        if u == U - 4 and layer + 1 < DEPTH:
                            tr_norm(layer + 1, *PE_NEXT[1:])
                        for v in range(u, u + size):
                            multiply(layer * U + v, [1])
                    u += size


_INS = ["x", "attn_norm", "ffn_norm", "w_in", "b_gate", "b_forget", "pool_w", "pool_scale", "diff_q_norm",
        "diff_k_norm", "diff_subln", "lam_q1", "lam_k1", "lam_q2", "lam_k2", "fox_q_norm", "fox_k_norm",
        "w_branch", "w_out", "w_ffn_up", "w_ffn_down"]


def kernel(**inputs):
    import concourse.bacc as _bacc
    from concourse.bass_utils import run_bass_kernel_spmd as _run

    nc = _bacc.Bacc("TRN2", target_bir_lowering=False, num_devices=1)
    arrays, args = {}, []
    for name in _INS:
        a = np.ascontiguousarray(inputs[name])
        arrays[f"in_{name}_dram"] = a
        args.append(nc.dram_tensor(f"in_{name}_dram", a.shape, mybir.dt.from_np(a.dtype), kind="ExternalInput").ap())
    consts = np.concatenate(list(constant_blocks().values()), axis=1)
    arrays["consts_dram"] = consts
    args.append(nc.dram_tensor("consts_dram", consts.shape, F32, kind="ExternalInput").ap())
    args.append(nc.dram_tensor("out_dram", (1, SEQ, D), F32, kind="ExternalOutput").ap())
    build(nc, *args)
    r = _run(nc, [arrays], core_ids=[0])
    return r.results[0]["out_dram"]
```
